# Optimizing a Trainium2 kernel written in Bass

```python
import math
import jax
import jax.numpy as jnp
from jax import lax
import numpy as np

D_MODEL = 1024
BATCH = 1
SEQ = 256
DEPTH = 1

MIX_WIDTH = D_MODEL
MLSTM_WIDTH = MIX_WIDTH // 2
MLSTM_HEADS = 4
MLSTM_HEAD_DIM = MLSTM_WIDTH // MLSTM_HEADS
MLSTM_CHUNK = 128
MLSTM_M_INIT = -1e30
HYENA_WIDTH = MIX_WIDTH - MLSTM_WIDTH
HYENA_GROUPS = 4
HYENA_GROUP_DIM = HYENA_WIDTH // HYENA_GROUPS
HYENA_ORDER = 2
HYENA_DIRS = 2
HYENA_BANDS = 16
HYENA_EMB_DIM = 1 + 2 * HYENA_BANDS
HYENA_FILTER_HIDDEN = 64
HYENA_WINDOW_SHIFT = 0.05
HYENA_SLOW_DECAY = -math.log(1e-2) / 1.5
HYENA_FAST_DECAY = -math.log(1e-2) / 0.3
SHORT_CONV = 3
N_GATE_COLS = 4 * MLSTM_HEADS
PROJ_COLS = 4 * MLSTM_WIDTH + N_GATE_COLS + (HYENA_ORDER + 1) * HYENA_WIDTH
N_EXPERTS = 16
EC_CAPACITY_FACTOR = 2
EXPERT_FF = 2 * D_MODEL
RMS_EPS = 1e-6


def rms_norm(x, g):
    xf = x.astype(jnp.float32)
    y = xf * lax.rsqrt(jnp.mean(xf * xf, axis=-1, keepdims=True) + RMS_EPS)
    return (y * g.astype(jnp.float32)).astype(x.dtype)

def centred_short_conv(u, w, b):
    S = u.shape[1]
    r = SHORT_CONV // 2
    up = jnp.pad(u, ((0, 0), (r, r), (0, 0)))
    y = b
    for j in range(SHORT_CONV):
        y = y + up[:, j:j + S] * w[j]
    return y

def mlstm_scan(q, k, v, i_pre, logf):
    B, H, S, Dh = q.shape
    nc = S // MLSTM_CHUNK
    qc = q.reshape(B, H, nc, MLSTM_CHUNK, Dh)
    kc = k.reshape(B, H, nc, MLSTM_CHUNK, Dh)
    vc = v.reshape(B, H, nc, MLSTM_CHUNK, Dh)
    ic = i_pre.reshape(B, H, nc, MLSTM_CHUNK)
    b = jnp.cumsum(logf.reshape(B, H, nc, MLSTM_CHUNK), axis=-1)
    g = b[..., -1]
    w_end = g[..., None] - b + ic
    a = jnp.max(w_end, axis=-1)
    e_end = jnp.exp(w_end - a[..., None])
    c_loc = jnp.einsum('bhcsv,bhcsk->bhcvk', vc * e_end[..., None], kc)
    n_loc = jnp.einsum('bhcs,bhcsk->bhck', e_end, kc)

    def step(carry, inp):
        c_st, n_st, m_st = carry
        g_j, a_j, c_j, n_j = inp
        m_new = jnp.maximum(g_j + m_st, a_j)
        s_prev = jnp.exp(g_j + m_st - m_new)
        s_loc = jnp.exp(a_j - m_new)
        c_new = s_prev[..., None, None] * c_st + s_loc[..., None, None] * c_j
        n_new = s_prev[..., None] * n_st + s_loc[..., None] * n_j
        return (c_new, n_new, m_new), (c_st, n_st, m_st)

    init = (jnp.zeros((B, H, Dh, Dh), q.dtype), jnp.zeros((B, H, Dh), q.dtype),
            jnp.full((B, H), MLSTM_M_INIT, q.dtype))
    xs = tuple(jnp.moveaxis(t, 2, 0) for t in (g, a, c_loc, n_loc))
    _, (c_in, n_in, m_in) = lax.scan(step, init, xs)
    c_in = jnp.moveaxis(c_in, 0, 2)
    n_in = jnp.moveaxis(n_in, 0, 2)
    m_in = jnp.moveaxis(m_in, 0, 2)

    tri = jnp.tril(jnp.ones((MLSTM_CHUNK, MLSTM_CHUNK), dtype=bool))
    log_d = jnp.where(tri, b[..., :, None] - b[..., None, :] + ic[..., None, :], -jnp.inf)
    log_inter = b + m_in[..., None]
    m_t = jnp.maximum(log_inter, jnp.max(log_d, axis=-1))
    d = jnp.exp(log_d - m_t[..., None])
    e_inter = jnp.exp(log_inter - m_t)
    s = jnp.einsum('bhctd,bhcsd->bhcts', qc, kc) * d
    num = (jnp.einsum('bhcts,bhcsd->bhctd', s, vc)
           + e_inter[..., None] * jnp.einsum('bhcvk,bhctk->bhctv', c_in, qc))
    den = jnp.sum(s, axis=-1) + e_inter * jnp.einsum('bhck,bhctk->bhct', n_in, qc)
    nrm = jnp.maximum(jnp.abs(den), jnp.exp(-m_t))
    return (num / nrm[..., None]).reshape(B, H, S, Dh)

def mlstm_mixer(q, k, v, o, gates, conv_w, conv_b, norm_g):
    B, S, _ = q.shape
    H, Dh = MLSTM_HEADS, MLSTM_HEAD_DIM
    qk = jax.nn.silu(centred_short_conv(jnp.concatenate([q, k], axis=-1), conv_w, conv_b))
    q, k = jnp.split(qk, 2, axis=-1)

    def heads(t):
        return t.reshape(B, S, H, Dh).transpose(0, 2, 1, 3).astype(jnp.float32)

    qh, kh, vh = heads(q), heads(k) * (MLSTM_HEAD_DIM ** -0.5), heads(v)
    g4 = gates.reshape(B, S, 4, H).transpose(2, 0, 3, 1).astype(jnp.float32)
    i_f, f_f, i_b, f_b = g4[0], g4[1], g4[2], g4[3]
    h_f = mlstm_scan(qh, kh, vh, i_f, jax.nn.log_sigmoid(f_f))

    def fl(t):
        return jnp.flip(t, axis=2)

    h_b = fl(mlstm_scan(fl(qh), fl(kh), fl(vh), fl(i_b), fl(jax.nn.log_sigmoid(f_b))))
    hsum = (h_f + h_b).transpose(0, 2, 1, 3)
    hn = rms_norm(hsum, norm_g.reshape(H, Dh)).reshape(B, S, MLSTM_WIDTH)
    return (jax.nn.sigmoid(o.astype(jnp.float32)) * hn).astype(o.dtype)

def hyena_filters(L, w1, b1, w2, b2, w3, freq, deltas):
    f32 = jnp.float32
    t = jnp.linspace(0.0, 1.0, L, dtype=f32)[:, None]
    w = 2.0 * math.pi * jnp.arange(L, dtype=f32)[:, None] / L
    bands = jnp.linspace(1e-4, HYENA_BANDS - 1, HYENA_BANDS, dtype=f32)[None, :]
    z = jnp.concatenate([t, jnp.cos(bands * w), -jnp.sin(bands * w)], axis=-1)
    fr = freq.astype(f32)
    hid = jnp.sin(fr * (z @ w1.astype(f32) + b1.astype(f32)))
    hid = jnp.sin(fr * (hid @ w2.astype(f32) + b2.astype(f32)))
    h = hid @ w3.astype(f32)
    window = jnp.exp(-t * jnp.abs(deltas.astype(f32))) + HYENA_WINDOW_SHIFT
    return (h * window).reshape(L, HYENA_ORDER, HYENA_DIRS, HYENA_WIDTH)

def bidir_long_conv(u, h_fwd, h_bwd, bias):
    L, C = h_fwd.shape
    two_sided = jnp.concatenate([(h_fwd[0] + h_bwd[0])[None], h_fwd[1:],
                                 jnp.zeros((1, C), jnp.float32), jnp.flip(h_bwd[1:], axis=0)], axis=0)
    k_f = jnp.fft.rfft(two_sided, n=2 * L, axis=0)
    uf = u.astype(jnp.float32)
    u_f = jnp.fft.rfft(uf, n=2 * L, axis=1)
    y = jnp.fft.irfft(u_f * k_f[None], n=2 * L, axis=1)[:, :L]
    return (y + uf * bias.astype(jnp.float32)).astype(u.dtype)

def hyena_mixer(hx, conv_w, conv_b, filt, bias, norm_g):
    B, S, _ = hx.shape
    u = centred_short_conv(hx, conv_w, conv_b)
    x1, x2, z = jnp.split(u, HYENA_ORDER + 1, axis=-1)
    z = x1 * bidir_long_conv(z, filt[:, 0, 0], filt[:, 0, 1], bias[0])
    z = x2 * bidir_long_conv(z, filt[:, 1, 0], filt[:, 1, 1], bias[1])
    zg = z.reshape(B, S, HYENA_GROUPS, HYENA_GROUP_DIM)
    return rms_norm(zg, norm_g.reshape(HYENA_GROUPS, HYENA_GROUP_DIM)).reshape(B, S, HYENA_WIDTH)

def expert_choice_moe(xn, w_router, w_gate, w_up, w_down):
    B, T, D = xn.shape
    cap = EC_CAPACITY_FACTOR * T // N_EXPERTS
    aff = jax.nn.softmax((xn @ w_router).astype(jnp.float32), axis=-1)
    g, idx = lax.top_k(jnp.swapaxes(aff, 1, 2), cap)
    bidx = jnp.arange(B)[:, None, None]
    xs = xn[bidx, idx]
    hid = jax.nn.silu(jnp.einsum('becd,edf->becf', xs, w_gate)) * jnp.einsum('becd,edf->becf', xs, w_up)
    y = jnp.einsum('becf,efd->becd', hid, w_down) * g[..., None].astype(xn.dtype)
    return jnp.zeros_like(xn).at[bidx, idx].add(y)

def first_inputs(seed: int = 0) -> dict:
    key = jax.random.key(seed)
    ks = jax.random.split(key, 32)
    f32 = jnp.float32
    D, L = D_MODEL, DEPTH

    def nrm(k, shape, scale):
        return jax.random.normal(k, shape, f32) * scale

    gate_off = 4 * MLSTM_WIDTH
    H = MLSTM_HEADS
    f_bias = jnp.linspace(3.0, 6.0, H, dtype=f32)
    b_in = nrm(ks[5], (L, PROJ_COLS), 0.02)
    b_in = b_in.at[:, gate_off + H:gate_off + 2 * H].add(f_bias)
    b_in = b_in.at[:, gate_off + 3 * H:gate_off + 4 * H].add(f_bias)
    n_filt = HYENA_ORDER * HYENA_DIRS * HYENA_WIDTH
    base_delta = jnp.tile(jnp.linspace(HYENA_SLOW_DECAY, HYENA_FAST_DECAY, HYENA_WIDTH, dtype=f32),
                          HYENA_ORDER * HYENA_DIRS)
    return {
        'x': nrm(ks[0], (BATCH, SEQ, D), 1.0),
        'c': nrm(ks[1], (BATCH, D), 1.0),
        'w_ada': nrm(ks[2], (L, D, 6 * D), 0.5 * D ** -0.5),
        'b_ada': nrm(ks[3], (L, 6 * D), 0.02),
        'g_mix': 1.0 + nrm(ks[4], (L, D), 0.02),
        'w_in': nrm(ks[6], (L, D, PROJ_COLS), D ** -0.5),
        'b_in': b_in,
        'conv_qk_w': nrm(ks[7], (L, SHORT_CONV, 2 * MLSTM_WIDTH), SHORT_CONV ** -0.5),
        'conv_qk_b': nrm(ks[8], (L, 2 * MLSTM_WIDTH), 0.02),
        'mlstm_norm_g': 1.0 + nrm(ks[9], (L, MLSTM_WIDTH), 0.02),
        'conv_hy_w': nrm(ks[10], (L, SHORT_CONV, (HYENA_ORDER + 1) * HYENA_WIDTH), SHORT_CONV ** -0.5),
        'conv_hy_b': nrm(ks[11], (L, (HYENA_ORDER + 1) * HYENA_WIDTH), 0.02),
        'hy_w1': nrm(ks[12], (L, HYENA_EMB_DIM, HYENA_FILTER_HIDDEN), HYENA_EMB_DIM ** -0.5),
        'hy_b1': nrm(ks[13], (L, HYENA_FILTER_HIDDEN), 0.1),
        'hy_w2': nrm(ks[14], (L, HYENA_FILTER_HIDDEN, HYENA_FILTER_HIDDEN), HYENA_FILTER_HIDDEN ** -0.5),
        'hy_b2': nrm(ks[15], (L, HYENA_FILTER_HIDDEN), 0.1),
        'hy_w3': nrm(ks[16], (L, HYENA_FILTER_HIDDEN, n_filt), 0.1 * HYENA_FILTER_HIDDEN ** -0.5),
        'hy_freq': 1.0 + nrm(ks[17], (L, HYENA_FILTER_HIDDEN), 0.02),
        'hy_deltas': base_delta[None] * (1.0 + nrm(ks[18], (L, n_filt), 0.02)),
        'hy_bias': nrm(ks[19], (L, HYENA_ORDER, HYENA_WIDTH), 0.1),
        'hyena_norm_g': 1.0 + nrm(ks[20], (L, HYENA_WIDTH), 0.02),
        'w_out': nrm(ks[21], (L, MIX_WIDTH, D), MIX_WIDTH ** -0.5),
        'g_ffn': 1.0 + nrm(ks[22], (L, D), 0.02),
        'w_router': nrm(ks[23], (L, D, N_EXPERTS), D ** -0.5),
        'w_gate': nrm(ks[24], (L, N_EXPERTS, D, EXPERT_FF), D ** -0.5),
        'w_up': nrm(ks[25], (L, N_EXPERTS, D, EXPERT_FF), D ** -0.5),
        'w_down': nrm(ks[26], (L, N_EXPERTS, EXPERT_FF, D), EXPERT_FF ** -0.5),
        'g_final': 1.0 + nrm(ks[27], (D,), 0.02),
    }

def first_block(x, c, w_ada, b_ada, g_mix, w_in, b_in, conv_qk_w, conv_qk_b, mlstm_norm_g,
              conv_hy_w, conv_hy_b, hy_w1, hy_b1, hy_w2, hy_b2, hy_w3, hy_freq, hy_deltas, hy_bias,
              hyena_norm_g, w_out, g_ffn, w_router, w_gate, w_up, w_down, g_final):
    W = MLSTM_WIDTH
    split_pts = [W, 2 * W, 3 * W, 4 * W, 4 * W + N_GATE_COLS]
    seq_len = x.shape[1]
    for l in range(DEPTH):
        mod = (c @ w_ada[l] + b_ada[l])[:, None, :]
        sh1, sc1, gt1, sh2, sc2, gt2 = jnp.split(mod, 6, axis=-1)
        h = rms_norm(x, g_mix[l]) * (1 + sc1) + sh1
        p = h @ w_in[l] + b_in[l]
        q, k, v, o, gates, hx = jnp.split(p, split_pts, axis=-1)
        y_m = mlstm_mixer(q, k, v, o, gates, conv_qk_w[l], conv_qk_b[l], mlstm_norm_g[l])
        filt = hyena_filters(seq_len, hy_w1[l], hy_b1[l], hy_w2[l], hy_b2[l], hy_w3[l], hy_freq[l], hy_deltas[l])
        y_h = hyena_mixer(hx, conv_hy_w[l], conv_hy_b[l], filt, hy_bias[l], hyena_norm_g[l])
        mixed = jnp.concatenate([y_m, y_h], axis=-1) @ w_out[l]
        x = x + gt1 * mixed
        hf = rms_norm(x, g_ffn[l]) * (1 + sc2) + sh2
        x = x + gt2 * expert_choice_moe(hf, w_router[l], w_gate[l], w_up[l], w_down[l])
    return rms_norm(x, g_final)


DEPTH_2 = 2

CTX_LEN = 256
GRID_W = 64
HEAD_DIM = 64

NA_HEADS = 6
NA_WIN_ROWS = 8
NA_WIN_COLS = 16

GLA_HEADS = 4
GLA_DK = 32
GLA_DV = 64
GLA_RANK = 16
GLA_GATE_NORM = 16.0
GLA_CHUNK = 64

GQA_Q_HEADS = 6
GQA_KV_HEADS = 2
GQA_REP = GQA_Q_HEADS // GQA_KV_HEADS
Q_BLOCK = 128
ROPE_THETA = 10000.0
ROPE_AXIS_PAIRS = HEAD_DIM // 4

FFN_HIDDEN = ((8 * D_MODEL + 3 * 256 - 1) // (3 * 256)) * 256

NA_W = NA_HEADS * HEAD_DIM
GLA_KW = GLA_HEADS * GLA_DK
GLA_VW = GLA_HEADS * GLA_DV
GQA_QW = GQA_Q_HEADS * HEAD_DIM
GQA_KVW = GQA_KV_HEADS * HEAD_DIM
MIX_W = NA_W + GLA_VW + GQA_QW
IN_WIDTHS = (NA_W, NA_W, NA_W, GLA_KW, GLA_KW, GLA_VW, GLA_VW, 2 * GLA_RANK, GQA_QW, GQA_KVW, GQA_KVW)
IN_COLS = sum(IN_WIDTHS)
IN_SPLITS = [int(s) for s in np.cumsum(IN_WIDTHS)[:-1]]

DEEPNORM_ALPHA = (2.0 * DEPTH_2) ** 0.25
DEEPNORM_BETA = (8.0 * DEPTH_2) ** -0.25
LN_EPS = 1e-5


def layer_norm(x, g, b):
    xf = x.astype(jnp.float32)
    mu = jnp.mean(xf, axis=-1, keepdims=True)
    var = jnp.mean(jnp.square(xf - mu), axis=-1, keepdims=True)
    return ((xf - mu) * lax.rsqrt(var + LN_EPS) * g + b).astype(x.dtype)

def rms_norm_2(x, w):
    xf = x.astype(jnp.float32)
    ms = jnp.mean(jnp.square(xf), axis=-1, keepdims=True)
    return (xf * lax.rsqrt(ms + RMS_EPS) * w).astype(x.dtype)

def modulate(x, shift, scale):
    return x * (1 + scale) + shift

def to_heads(t, n_heads):
    b, n, _ = t.shape
    return t.reshape(b, n, n_heads, -1).transpose(0, 2, 1, 3)

def merge_heads(t):
    b, h, n, d = t.shape
    return t.transpose(0, 2, 1, 3).reshape(b, n, h * d)

def flip_seq(t):
    return jnp.flip(t, axis=2)

def axial_rope_tables(n_tokens):
    t = jnp.arange(n_tokens)
    row = (t // GRID_W).astype(jnp.float32)
    col = (t % GRID_W).astype(jnp.float32)
    inv_freq = ROPE_THETA ** (-jnp.arange(ROPE_AXIS_PAIRS, dtype=jnp.float32) / ROPE_AXIS_PAIRS)
    ang_r = row[:, None] * inv_freq
    ang_c = col[:, None] * inv_freq
    ang = jnp.concatenate([ang_r, ang_r, ang_c, ang_c], axis=-1)
    return jnp.cos(ang), jnp.sin(ang)

def apply_axial_rope(x, cos, sin):
    xf = x.astype(jnp.float32)
    x1, x2, x3, x4 = jnp.split(xf, 4, axis=-1)
    rot = jnp.concatenate([-x2, x1, -x4, x3], axis=-1)
    return (xf * cos + rot * sin).astype(x.dtype)

def context_attention(q, k, v):
    s = jnp.einsum('bgrqd,bgkd->bgrqk', q, k, preferred_element_type=jnp.float32) * (q.shape[-1] ** -0.5)
    p = jax.nn.softmax(s, axis=-1).astype(v.dtype)
    return jnp.einsum('bgrqk,bgkd->bgrqd', p, v)

def neighborhood_attention(q, k, v, k_ctx, v_ctx, rpb):
    B, H, N, d = q.shape
    rows = N // GRID_W
    wr = min(NA_WIN_ROWS, rows)
    scale = d ** -0.5
    qg = q.reshape(B, H, rows, GRID_W, d)
    kg = k.reshape(B, H, rows, GRID_W, d)
    vg = v.reshape(B, H, rows, GRID_W, d)
    cols = jnp.arange(GRID_W)
    col_start = jnp.clip(cols - NA_WIN_COLS // 2, 0, GRID_W - NA_WIN_COLS)
    col_in = (cols[None, :] >= col_start[:, None]) & (cols[None, :] < col_start[:, None] + NA_WIN_COLS)
    dc_idx = jnp.clip(cols[None, :] - cols[:, None], -(NA_WIN_COLS - 1), NA_WIN_COLS - 1) + (NA_WIN_COLS - 1)

    def row_block(r):
        rs = jnp.clip(r - wr // 2, 0, rows - wr)
        q_r = lax.dynamic_index_in_dim(qg, r, axis=2, keepdims=False)
        k_s = lax.dynamic_slice_in_dim(kg, rs, wr, axis=2)
        v_s = lax.dynamic_slice_in_dim(vg, rs, wr, axis=2)
        dr_idx = rs + jnp.arange(wr) - r + (NA_WIN_ROWS - 1)
        bias = rpb[:, dr_idx[None, :, None], dc_idx[:, None, :]]
        s_lat = jnp.einsum('bhqd,bhrkd->bhqrk', q_r, k_s, preferred_element_type=jnp.float32) * scale + bias.astype(jnp.float32)
        s_lat = jnp.where(col_in[:, None, :], s_lat, -jnp.inf).reshape(B, H, GRID_W, wr * GRID_W)
        s_ctx = jnp.einsum('bhqd,bhcd->bhqc', q_r, k_ctx, preferred_element_type=jnp.float32) * scale
        p = jax.nn.softmax(jnp.concatenate([s_lat, s_ctx], axis=-1), axis=-1).astype(v.dtype)
        p_lat = p[..., : wr * GRID_W].reshape(B, H, GRID_W, wr, GRID_W)
        p_ctx = p[..., wr * GRID_W:]
        return jnp.einsum('bhqrk,bhrkd->bhqd', p_lat, v_s) + jnp.einsum('bhqc,bhcd->bhqd', p_ctx, v_ctx)

    o = lax.map(row_block, jnp.arange(rows))
    return o.transpose(1, 2, 0, 3, 4).reshape(B, H, N, d)

def gqa_latent_attention(q, k, v, k_ctx, v_ctx):
    B, G, R, N, d = q.shape
    nb = N // Q_BLOCK
    keys = jnp.concatenate([k, k_ctx], axis=2)
    vals = jnp.concatenate([v, v_ctx], axis=2)
    qb = q.reshape(B, G, R, nb, Q_BLOCK, d).transpose(3, 0, 1, 2, 4, 5)

    def block(q_blk):
        s = jnp.einsum('bgrqd,bgkd->bgrqk', q_blk, keys, preferred_element_type=jnp.float32) * (d ** -0.5)
        p = jax.nn.softmax(s, axis=-1).astype(vals.dtype)
        return jnp.einsum('bgrqk,bgkd->bgrqd', p, vals)

    o = lax.map(block, qb)
    return o.transpose(1, 2, 3, 0, 4, 5).reshape(B, G * R, N, d)

def gla_log_gates(lr, wa2, ba):
    B, N, _ = lr.shape
    z = jnp.einsum('bner,erk->ebnk', lr.reshape(B, N, 2, GLA_RANK), wa2) + ba[:, None, None, :]
    la = jax.nn.log_sigmoid(z.astype(jnp.float32)) / GLA_GATE_NORM
    la = la.reshape(2, B, N, GLA_HEADS, GLA_DK).transpose(0, 1, 3, 2, 4)
    return la[0], la[1]

def gla_chunked(q, k, v, log_a, s0):
    B, H, N, dk = q.shape
    dv = v.shape[-1]
    nc = N // GLA_CHUNK

    def to_chunks(t):
        return t.astype(jnp.float32).reshape(B, H, nc, GLA_CHUNK, t.shape[-1]).transpose(2, 0, 1, 3, 4)

    causal = jnp.tril(jnp.ones((GLA_CHUNK, GLA_CHUNK), dtype=bool))

    def step(S, xs):
        qi, ki, vi, gi = xs
        b = jnp.cumsum(gi, axis=-2)
        b_last = b[..., -1:, :]
        diff = b[..., :, None, :] - b[..., None, :, :]
        decay = jnp.exp(jnp.where(causal[:, :, None], diff, -jnp.inf))
        A = jnp.einsum('bhtd,bhsd,bhtsd->bhts', qi, ki, decay)
        o = jnp.einsum('bhts,bhsv->bhtv', A, vi) + jnp.einsum('bhtd,bhdv->bhtv', qi * jnp.exp(b), S)
        S = jnp.exp(b_last)[..., 0, :, None] * S + jnp.einsum('bhsd,bhsv->bhdv', ki * jnp.exp(b_last - b), vi)
        return S, o

    S, o = lax.scan(step, s0.astype(jnp.float32), (to_chunks(q), to_chunks(k), to_chunks(v), to_chunks(log_a)))
    return o.transpose(1, 2, 0, 3, 4).reshape(B, H, N, dv).astype(v.dtype), S

def gla_final_state(k, v, log_a):
    b = jnp.cumsum(log_a.astype(jnp.float32), axis=2)
    w = jnp.exp(b[:, :, -1:, :] - b)
    return jnp.einsum('bhsd,bhsv->bhdv', k.astype(jnp.float32) * w, v.astype(jnp.float32))

def gla_bidirectional(q, k, v, la_f, la_b, s_f, s_b):
    o_f, s_f_end = gla_chunked(q, k, v, la_f, s_f)
    o_b, s_b_end = gla_chunked(flip_seq(q), flip_seq(k), flip_seq(v), flip_seq(la_b), s_b)
    return o_f + flip_seq(o_b), s_f_end, s_b_end

def gla_output(o, norm_w, g):
    return merge_heads(rms_norm_2(o, norm_w)) * jax.nn.silu(g)

def token_mixers(u, uc, w_in, rpb, gla_wa2, gla_ba, gla_norm_w, q_norm_w, k_norm_w, rope_cos, rope_sin, ctx_out):
    B, N, _ = u.shape
    (na_q, na_k, na_v, gl_q, gl_k, gl_v, gl_g, gl_lr, ga_q, ga_k, ga_v) = jnp.split(u @ w_in, IN_SPLITS, axis=-1)
    (na_qc, na_kc, na_vc, gl_qc, gl_kc, gl_vc, gl_gc, gl_lrc, ga_qc, ga_kc, ga_vc) = jnp.split(uc @ w_in, IN_SPLITS, axis=-1)

    k_na_c = to_heads(na_kc, NA_HEADS)
    v_na_c = to_heads(na_vc, NA_HEADS)
    o_na = neighborhood_attention(to_heads(na_q, NA_HEADS), to_heads(na_k, NA_HEADS), to_heads(na_v, NA_HEADS), k_na_c, v_na_c, rpb)

    la_f, la_b = gla_log_gates(gl_lr, gla_wa2, gla_ba)
    la_fc, la_bc = gla_log_gates(gl_lrc, gla_wa2, gla_ba)
    k_gl_c = to_heads(gl_kc, GLA_HEADS)
    v_gl_c = to_heads(gl_vc, GLA_HEADS)
    if ctx_out:
        s0 = jnp.zeros((B, GLA_HEADS, GLA_DK, GLA_DV), jnp.float32)
        q_gl_c = to_heads(gl_qc, GLA_HEADS) * GLA_DK ** -0.5
        oc_gl, s_f, s_b = gla_bidirectional(q_gl_c, k_gl_c, v_gl_c, la_fc, la_bc, s0, s0)
    else:
        s_f = gla_final_state(k_gl_c, v_gl_c, la_fc)
        s_b = gla_final_state(flip_seq(k_gl_c), flip_seq(v_gl_c), flip_seq(la_bc))
    o_gl, _, _ = gla_bidirectional(to_heads(gl_q, GLA_HEADS) * GLA_DK ** -0.5, to_heads(gl_k, GLA_HEADS), to_heads(gl_v, GLA_HEADS), la_f, la_b, s_f, s_b)

    q_ga = apply_axial_rope(rms_norm_2(to_heads(ga_q, GQA_Q_HEADS), q_norm_w), rope_cos, rope_sin)
    k_ga = apply_axial_rope(rms_norm_2(to_heads(ga_k, GQA_KV_HEADS), k_norm_w), rope_cos, rope_sin)
    k_ga_c = rms_norm_2(to_heads(ga_kc, GQA_KV_HEADS), k_norm_w)
    v_ga_c = to_heads(ga_vc, GQA_KV_HEADS)
    o_ga = gqa_latent_attention(q_ga.reshape(B, GQA_KV_HEADS, GQA_REP, N, HEAD_DIM), k_ga, to_heads(ga_v, GQA_KV_HEADS), k_ga_c, v_ga_c)

    o = jnp.concatenate([merge_heads(o_na), gla_output(o_gl, gla_norm_w, gl_g), merge_heads(o_ga)], axis=-1)
    if not ctx_out:
        return o, None

    L = uc.shape[1]
    oc_na = context_attention(to_heads(na_qc, NA_HEADS)[:, :, None], k_na_c, v_na_c)[:, :, 0]
    q_ga_c = rms_norm_2(to_heads(ga_qc, GQA_Q_HEADS), q_norm_w).reshape(B, GQA_KV_HEADS, GQA_REP, L, HEAD_DIM)
    oc_ga = context_attention(q_ga_c, k_ga_c, v_ga_c).reshape(B, GQA_Q_HEADS, L, HEAD_DIM)
    oc = jnp.concatenate([merge_heads(oc_na), gla_output(oc_gl, gla_norm_w, gl_gc), merge_heads(oc_ga)], axis=-1)
    return o, oc

def swiglu(u, w_ffn_in, w_ffn_out):
    a, b = jnp.split(u @ w_ffn_in, 2, axis=-1)
    return (jax.nn.silu(a) * b) @ w_ffn_out

def second_inputs(seed: int = 0) -> dict:
    key = jax.random.key(seed)
    ks = jax.random.split(key, 20)

    def nrm(k, shape, scale):
        return jax.random.normal(k, shape, jnp.float32) * scale

    L = DEPTH_2
    return {
        'x': nrm(ks[0], (BATCH, SEQ, D_MODEL), 1.0),
        'c': nrm(ks[1], (BATCH, D_MODEL), 1.0),
        'ctx': nrm(ks[2], (BATCH, CTX_LEN, D_MODEL), 1.0),
        'c_ctx': nrm(ks[3], (D_MODEL,), 1.0),
        'w_ada': nrm(ks[4], (L, D_MODEL, 6 * D_MODEL), 0.5 * D_MODEL ** -0.5),
        'b_ada': nrm(ks[5], (L, 6 * D_MODEL), 0.02),
        'w_in': nrm(ks[6], (L, D_MODEL, IN_COLS), D_MODEL ** -0.5),
        'na_rpb': nrm(ks[7], (L, NA_HEADS, 2 * NA_WIN_ROWS - 1, 2 * NA_WIN_COLS - 1), 0.1),
        'gla_wa2': nrm(ks[8], (L, 2, GLA_RANK, GLA_KW), GLA_RANK ** -0.5),
        'gla_ba': nrm(ks[9], (L, 2, GLA_KW), 0.02),
        'gla_norm_w': 1.0 + nrm(ks[10], (L, GLA_DV), 0.05),
        'gqa_qnorm_w': 1.0 + nrm(ks[11], (L, HEAD_DIM), 0.05),
        'gqa_knorm_w': 1.0 + nrm(ks[12], (L, HEAD_DIM), 0.05),
        'w_out': nrm(ks[13], (L, MIX_W, D_MODEL), DEEPNORM_BETA * MIX_W ** -0.5),
        'ln1_g': 1.0 + nrm(ks[14], (L, D_MODEL), 0.05),
        'ln1_b': nrm(ks[15], (L, D_MODEL), 0.02),
        'w_ffn_in': nrm(ks[16], (L, D_MODEL, 2 * FFN_HIDDEN), D_MODEL ** -0.5),
        'w_ffn_out': nrm(ks[17], (L, FFN_HIDDEN, D_MODEL), DEEPNORM_BETA * FFN_HIDDEN ** -0.5),
        'ln2_g': 1.0 + nrm(ks[18], (L, D_MODEL), 0.05),
        'ln2_b': nrm(ks[19], (L, D_MODEL), 0.02),
    }

def second_block(x, c, ctx, c_ctx, w_ada, b_ada, w_in, na_rpb, gla_wa2, gla_ba, gla_norm_w, gqa_qnorm_w, gqa_knorm_w, w_out, ln1_g, ln1_b, w_ffn_in, w_ffn_out, ln2_g, ln2_b):
    rope_cos, rope_sin = axial_rope_tables(x.shape[1])
    silu_c = jax.nn.silu(c)
    silu_cc = jax.nn.silu(c_ctx)
    xc = ctx
    for l in range(DEPTH_2):
        ctx_out = l < DEPTH_2 - 1
        mod = (silu_c @ w_ada[l] + b_ada[l])[:, None, :]
        mod_c = silu_cc @ w_ada[l] + b_ada[l]
        sh1, sc1, g1, sh2, sc2, g2 = jnp.split(mod, 6, axis=-1)
        sh1c, sc1c, g1c, sh2c, sc2c, g2c = jnp.split(mod_c, 6, axis=-1)

        o, oc = token_mixers(modulate(x, sh1, sc1), modulate(xc, sh1c, sc1c), w_in[l], na_rpb[l], gla_wa2[l], gla_ba[l], gla_norm_w[l], gqa_qnorm_w[l], gqa_knorm_w[l], rope_cos, rope_sin, ctx_out)
        x = layer_norm(DEEPNORM_ALPHA * x + g1 * (o @ w_out[l]), ln1_g[l], ln1_b[l])
        x = layer_norm(DEEPNORM_ALPHA * x + g2 * swiglu(modulate(x, sh2, sc2), w_ffn_in[l], w_ffn_out[l]), ln2_g[l], ln2_b[l])
        if ctx_out:
            xc = layer_norm(DEEPNORM_ALPHA * xc + g1c * (oc @ w_out[l]), ln1_g[l], ln1_b[l])
            xc = layer_norm(DEEPNORM_ALPHA * xc + g2c * swiglu(modulate(xc, sh2c, sc2c), w_ffn_in[l], w_ffn_out[l]), ln2_g[l], ln2_b[l])
    return x


def setup_inputs(seed=0):
    out = dict(first_inputs(seed))
    for name, value in second_inputs(seed + 1).items():
        if name != "x":
            out[name + "_2"] = value
    return out


def reference(
    x, c, w_ada, b_ada, g_mix, w_in, b_in, conv_qk_w, conv_qk_b, mlstm_norm_g, conv_hy_w,
    conv_hy_b, hy_w1, hy_b1, hy_w2, hy_b2, hy_w3, hy_freq, hy_deltas, hy_bias, hyena_norm_g,
    w_out, g_ffn, w_router, w_gate, w_up, w_down, g_final, c_2, ctx_2, c_ctx_2, w_ada_2,
    b_ada_2, w_in_2, na_rpb_2, gla_wa2_2, gla_ba_2, gla_norm_w_2, gqa_qnorm_w_2, gqa_knorm_w_2,
    w_out_2, ln1_g_2, ln1_b_2, w_ffn_in_2, w_ffn_out_2, ln2_g_2, ln2_b_2,
):
    x = first_block(
        x, c, w_ada, b_ada, g_mix, w_in, b_in, conv_qk_w, conv_qk_b, mlstm_norm_g, conv_hy_w,
        conv_hy_b, hy_w1, hy_b1, hy_w2, hy_b2, hy_w3, hy_freq, hy_deltas, hy_bias, hyena_norm_g,
        w_out, g_ffn, w_router, w_gate, w_up, w_down, g_final,
    )
    return second_block(
        x, c_2, ctx_2, c_ctx_2, w_ada_2, b_ada_2, w_in_2, na_rpb_2, gla_wa2_2, gla_ba_2,
        gla_norm_w_2, gqa_qnorm_w_2, gqa_knorm_w_2, w_out_2, ln1_g_2, ln1_b_2, w_ffn_in_2,
        w_ffn_out_2, ln2_g_2, ln2_b_2,
    )


_drawn_inputs = setup_inputs


def setup_inputs(seed=0):
    import zlib

    import numpy as np

    out = dict(_drawn_inputs(seed))
    spreads = {}
    factors = {'g_mix': 4.938,
     'conv_qk_b': 23.071,
     'mlstm_norm_g': 8.0,
     'hy_freq': 3.54,
     'hyena_norm_g': 5.263,
     'g_ffn': 3.836,
     'g_final': 3.102,
     'ctx_2': 4.089,
     'b_ada_2': 5.517,
     'na_rpb_2': 64.0,
     'gla_wa2_2': 6.03,
     'gla_ba_2': 57.158,
     'gla_norm_w_2': 8.0,
     'gqa_qnorm_w_2': 8.0,
     'gqa_knorm_w_2': 8.0}
    for name, (base, spread) in spreads.items():
        noise = np.random.default_rng([zlib.crc32(name.encode()), seed]).standard_normal(out[name].shape)
        drawn = base * np.exp(spread * noise) if base else spread * noise
        out[name] = jnp.asarray(drawn.astype(out[name].dtype))
    for name, factor in factors.items():
        out[name] = (out[name] * factor).astype(out[name].dtype)
    return out
```

```python
from contextlib import ExitStack

import concourse.bass as bass
from concourse import mybir
import numpy as np

ALU = mybir.AluOpType
ACT = mybir.ActivationFunctionType
AX = mybir.AxisListType
F32 = mybir.dt.float32

P = 128
D = 1024
KD = D // P
T = 256
TT = T // P
W = 512
H = 4
NG = 16
NE = 16
CAP = 2 * T // NE
FF = 2 * D
EPS = 1e-6
LN_EPS = 1e-5
NEG = -1e30
SLOT = 4096
RING = 4
ALPHA = 4.0 ** 0.25
NB = 8

TWO_PI = [6.28125, 8117 / 2 ** 22]
TWO_PI.append(2 * np.pi - sum(TWO_PI))

COLS1 = [("c", 8), ("b_ada", 48), ("g_mix", 8), ("conv_qk_w", 24), ("conv_qk_b", 8),
         ("mlstm_norm_g", 4), ("conv_hy_w", 36), ("conv_hy_b", 12), ("hy_bias", 8),
         ("hyena_norm_g", 4), ("g_ffn", 8), ("g_final", 8), ("b_qk", 8), ("b_o", 4), ("b_hx", 12)]
COLS2 = [("b_ada", 48), ("ln1_g", 8), ("ln1_b", 8), ("ln2_g", 8), ("ln2_b", 8), ("gla_norm", 1),
         ("qnorm", 1), ("knorm", 1), ("gla_ba", 2)]
COLS = COLS1 + [("c2", 16)] + [(f"{n}_{l}", w) for l in range(2) for n, w in COLS2]


def offsets(parts):
    at, out = 0, {}
    for name, width in parts:
        out[name] = (at, at + width)
        at += width
    return out, at


TABLES1 = [("ident", 128), ("ones", 128), ("tri_f", 128), ("tri_b", 128), ("neg_f", 128), ("neg_b", 128),
           ("before", 128), ("slots", CAP), ("dft_c", 512), ("dft_s", 512), ("dft_n", 256), ("idft_c", 512),
           ("idft_s", 512), ("minus_t", 2), ("eps", 1), ("ln_eps", 1), ("keep_im", 1), ("swap_im", 1), ("pick", 2)]
TABLES2 = [("half64", 128), ("flip64", 128), ("neg_col", 64), ("rope_c", 256), ("rope_s", 256),
           ("rope_r", 128), ("gla_lv", 160), ("diag32", 32), ("gla_bd", 256)]


def tables():
    f8 = np.float64
    i = np.arange(P)
    t = {}
    t["ident"] = np.eye(P)
    t["ones"] = np.ones((P, P))
    t["tri_f"] = (i[:, None] <= i[None, :])
    t["tri_b"] = (i[:, None] >= i[None, :])
    t["neg_f"] = np.where(i[None, :] <= i[:, None], 0, NEG)
    t["neg_b"] = np.where(i[None, :] >= i[:, None], 0, NEG)
    t["before"] = (i[None, :] < i[:, None])
    t["slots"] = np.tile(np.arange(CAP), (P, 1))
    s = np.arange(T, dtype=f8)
    ang = 2 * np.pi * np.outer(s, s) / (2 * T)

    def tiles(a):
        return a.reshape(TT, P, -1).transpose(1, 0, 2).reshape(P, -1)

    t["dft_c"] = tiles(np.cos(ang))
    t["dft_s"] = tiles(-np.sin(ang))
    ny = np.zeros((T, P))
    ny[:, 0] = (-1.0) ** s
    t["dft_n"] = tiles(ny)
    ic = 2 * np.cos(ang) / (2 * T)
    ic[0] /= 2
    js = -2 * np.sin(ang) / (2 * T)
    js[0] = (-1.0) ** s / (2 * T)
    t["idft_c"], t["idft_s"] = tiles(ic), tiles(js)
    t["minus_t"] = -np.linspace(0, 1, T, dtype=np.float32).reshape(TT, P).T
    t["eps"] = np.full((P, 1), EPS)
    t["ln_eps"] = np.full((P, 1), LN_EPS)
    t["keep_im"] = (i > 0)[:, None]
    t["swap_im"] = (i == 0)[:, None]
    t["pick"] = (i[:, None] % 32 == np.arange(2)[None])
    t["half64"] = (i[:, None] // 64 == i[None, :] // 64)
    t["flip64"] = (i[:, None] // 64 == i[None, :] // 64) & (i[:, None] % 64 + i[None, :] % 64 == 63)
    c = np.arange(64)
    c0 = np.clip(c - 8, 0, 48)
    t["neg_col"] = np.tile(np.where((c[None] >= c0[:, None]) & (c[None] < c0[:, None] + 16), 0, NEG), (2, 1))
    inv = 10000.0 ** (-np.arange(16, dtype=np.float32) / 16)
    ar, ac = (s // 64)[:, None] * inv, (s % 64)[:, None] * inv
    an = np.concatenate([ar, ar, ac, ac], 1).astype(np.float32).astype(f8)
    t["rope_c"], t["rope_s"] = np.tile(np.cos(an).T, (2, 1)), np.tile(np.sin(an).T, (2, 1))
    r = np.zeros((64, 64))
    for j in range(16):
        r[16 + j, j], r[j, 16 + j] = -1, 1
        r[48 + j, 32 + j], r[32 + j, 48 + j] = -1, 1
    t["rope_r"] = np.kron(np.eye(2), r)
    lv = []
    for m in (32, 16, 8, 4, 2):
        a, b = np.arange(P)[:, None] % 32, np.arange(32)[None]
        lv.append((a // m == b // m) & (a // (m // 2) != b // (m // 2)))
    t["gla_lv"] = np.concatenate(lv, 1)
    t["gla_bd"] = (i[:, None] // 32 == np.arange(T)[None] // 64)
    t["diag32"] = 2.0 * (np.arange(P)[:, None] % 32 == np.arange(32)[None])
    return [np.concatenate([t[n].astype(np.float32).reshape(P, w) for n, w in ts], 1) for ts in (TABLES1, TABLES2)]


def features():
    t = np.linspace(0.0, 1.0, T, dtype=np.float32)[:, None]
    w = (2.0 * np.pi * np.arange(T, dtype=np.float32)[:, None] / T).astype(np.float32)
    bands = np.linspace(1e-4, 15, 16, dtype=np.float32)[None]
    z = np.concatenate([t, np.cos(bands * w), -np.sin(bands * w)], -1)
    return np.ascontiguousarray(z.T.astype(np.float32))


def build(nc, I, out):
    ctx = ExitStack()
    with ctx:
        def sb(name, shape):
            return ctx.enter_context(nc.sbuf_tensor(name, shape, F32))

        def sem(name):
            return ctx.enter_context(nc.semaphore(name))

        pcol, n_cols = offsets(COLS)
        tcol, n_tab = offsets(TABLES1)
        tcol2, n_tab2 = offsets(TABLES2)
        ring = sb("ring", [P, RING, SLOT])
        par = sb("par", [P, n_cols])
        tab = sb("tab", [P, n_tab])
        XC = sb("XC", [P, KD, 2 * T])
        xT = XC[:, :, 0:T]
        arena = sb("arena", [P, 28700])

        def at(start, *shape):
            n = int(np.prod(shape))
            v = arena[:, start:start + n]
            if len(shape) == 2:
                v = v.rearrange("p (a b) -> p a b", b=shape[1])
            if len(shape) == 3:
                v = v.rearrange("p (a b c) -> p a b c", b=shape[1], c=shape[2])
            return v

        def pc(name, j=0, n=1):
            a = pcol[name][0] + j
            return par[:, a:a + n]

        def tb(name):
            return tab[:, slice(*tcol[name])]

        ident, ones = tb("ident"), tb("ones")
        dft = {n: tb(f"dft_{n}").rearrange("p (a b) -> p a b", a=TT) for n in "csn"}
        idft = {n: tb(f"idft_{n}").rearrange("p (a b) -> p a b", a=TT) for n in "cs"}
        tri = [tb("tri_f"), tb("tri_b")]
        neg = [tb("neg_f"), tb("neg_b")]

        def bc(ap, axis, *shape):
            return ap.unsqueeze(axis).to_broadcast([ap.shape[0], *shape])

        E = at(0, 4 * H, T)

        def KS(o, which, n, k=1):
            return at(((2 * o + which) * TT + n) * W, k * W)

        KR, KI = at(4096, 2 * TT, W), at(6144, 2 * TT, W)
        KB = at(8192, 2, W)
        hxp = at(9216, 12, T + 2)
        Y = at(9216, 2 * TT, W)
        ztok = at(11264, TT, W)
        qkp = at(12312, 8, T + 2)
        yT = at(12312, KD, T)
        hT = at(14376, KD, T)
        dlt = at(14376, 4 * W)
        qkT = at(16424, 8, T)
        w3 = at(16424, 4 * W)
        hxc = at(18472, 12, T)
        vtok = at(21544, TT, H, P + 1)
        hw1, hw2, hfe, hid, hhp = (at(21544, 64), at(21608, 64), at(21672, T), at(21928, T), at(22184, 4))
        hid2 = at(22192, T)
        sgo = at(22576, H, T)
        T1 = at(23600, 8 * T)
        win = at(23600, W)
        hwt = at(24112, 2, W)
        hs = at(25648, TT * H, P)
        bv = at(26672, W)
        bg = at(27184, NG)
        wg = at(27200, KD, NG)
        rs = at(27328, T)
        mod = at(27584, 48)
        A1 = at(27632, 8)
        G = at(27640, TT, NG)
        LF, AB, LG, FI, AC, MX, EM = (at(27672 + 16 * i, TT, 2, H) for i in range(7))
        MD, MF = at(27784, TT, 2, H), at(27800, TT, 2, H)
        dn = at(27816, 8)
        sst = at(27824, 8)
        rst = at(27832, 8)

        wr = at(27840, KD, NE)
        logit = at(27968, TT, NE)
        aff = at(28000, TT, NE)
        rank = at(28032, TT, NE)
        rpart = at(28064, TT, TT, NE)
        rmx = at(28128, TT)
        rsm = at(28130, TT)
        mod2early = at(28132, 2, 48, 2)
        cpad = at(28324, KD, 32)
        stages = {"ada": at(9216, 2, W), "ada0_": at(14376, 2, W), "ada1_": at(14376, 2, W)}
        sel = at(0, TT, NE, CAP)
        selg = at(1024, TT, NE, CAP)
        htok = at(2048, TT, D)
        diag = at(4096, NE, P)
        diags = [diag, at(23600, NE, P)]
        cmp_ = at(6144, 4, P)
        cmp2 = at(6656, 4, P)
        xs = at(7168, KD, NE * CAP)
        CT = at(11264, 4, T)
        xcur = at(16424, KD, P)
        sg = at(17448, 2, P)
        hidm = at(17704, 2, P)
        hdT = at(17960, 2, P)
        ysb = at(18216, D)
        T2 = at(23600, 8 * T)

        def tb2(name):
            return arena[:, slice(*tcol2[name])]

        lvmask = arena[:, tcol2["gla_lv"][0]:tcol2["diag32"][1]]
        wa2 = at(1664, 4, P).rearrange("p (l d) x -> p l d x", l=2)
        mod2s = at(1408, 2, 48, 2)
        A2, B2, AB_ = at(2272, 8, 2), at(2288, 8, 2), at(2312, 8)
        nm, sm = at(2304, 4), at(2308, 4)
        U = at(2400, KD, 2 * T)
        ex = at(2400, 2, 2 * T)
        hat = at(3424, 2, 2, T)
        AT = at(4448, 8, T)
        naq, nak, nav = at(6496, 3, 2 * T), at(8032, 3, 2 * T), at(9568, 4, 384)
        glq, glk, glv, glg = at(11104, 2 * T), at(11616, 2 * T), at(12128, 4, T), at(13152, 2, 2 * T)
        gllr, gaq, gav = at(14176, 2 * T), at(14688, 5, 2 * T), at(17248, 4, P)
        rtmp = gllr[:, 0:T]
        HID = at(6496, 22, 2 * T)
        oT = at(17760, KD, 2 * T)
        gsq, S0, grt, ktok = at(17760, 2, 2 * T), at(18784, 2, T), at(20320, 2, 2 * T), at(21344, 4, P)
        WW = at(21856, 42, 64)
        la, B, og, AB2 = at(24544, 2, 2 * T), at(25568, 2, 2 * T), at(26592, 2, 2 * T), at(26592, 2, 2 * T)
        dgt = at(24544, 448)
        sarg, khat, qe = at(27616, 4, T), at(27616, 2, T), at(28128, 2, T)
        Pr, PT = at(24544, 3, 2 * T), at(26080, 2, 4, P)
        mu, rs2, sga = at(24544, 2 * T), at(25056, 2 * T), at(25568, 2, 2 * T)

        ps = [ctx.enter_context(nc.psum_tensor(f"ps{b}", [P, 512], F32)) for b in range(NB)]
        full = [sem(f"full{b}") for b in range(NB)]
        free = [sem(f"free{b}") for b in range(NB)]

        place = {}

        def open_bank(pe, name):
            n = len(place)
            assert name not in place, name
            b, use = place[name] = (n % NB, n // NB)
            if use:
                pe.wait_ge(free[b], use)
            return ps[b]

        def close_bank(ins, name):
            ins.then_inc(full[place[name][0]], 1)

        def read_bank(eng, name):
            b, use = place[name]
            eng.wait_ge(full[b], use + 1)
            return ps[b]

        def chain(eng, own):
            said = {}

            def count(s):
                said[s.name] = said.get(s.name, 0) + 1
                return said[s.name]

            def step(ins, sem=None, frees=None):
                if frees is not None:
                    b, use = place[frees]
                    sem, value = free[b], use + 1
                else:
                    sem = sem or own
                    value = count(sem)
                ins.then_inc(sem, 1)
                eng.wait_ge(sem, value)

            def tell(sem):
                count(sem)
                eng.sem_inc(sem, 1)

            return step, tell


        s_x = sem("x_loaded")
        s_load = sem("tables_loaded")
        s_fil = sem("filter_inputs_loaded")
        s_row = sem("rows_loaded")
        landed = [sem(f"landed{i}") for i in range(RING)]
        drained = sem("slots_drained")
        act_own, dve_own = sem("act_step"), sem("dve_step")
        hid_ready, hid2_ready = sem("hid_ready"), sem("hid2_ready")
        arg_ready = sem("sine_argument_ready")
        win_ready, win_used = sem("window_ready"), sem("window_used")
        ks_ready, kspec_ready = sem("filters_ready"), sem("filter_spectra_ready")
        sq_ready, root_ready, h_ready = sem("squares_ready"), sem("roots_ready"), sem("h_ready")
        qk_evac, hx_evac, o_evac = sem("qk_evacuated"), sem("hx_evacuated"), sem("o_gate_ready")
        v_ready = sem("v_ready")
        conv_ready, qk_ready = sem("qk_convolved"), sem("qk_ready")
        z_ready, zt_ready, y_ready = sem("z_ready"), sem("z_by_token_ready"), sem("y_spectrum_ready")
        g_ready, g_exp, g_ln = sem("gates_ready"), sem("gates_exp"), sem("gates_log")
        lf_ready, diag_ready = sem("log_forget_ready"), sem("diagonals_ready")
        mx_ready, em_ready = sem("max_ready"), sem("exp_minus_max_ready")
        e_arg, e_ready, p_ready = sem("decay_argument"), sem("decay_ready"), sem("weights_ready")
        hs_ready, ss_ready, hn_ready = sem("h_summed"), sem("head_squares"), sem("h_normed")
        ym_ready, yh_ready = sem("y_mlstm_ready"), sem("y_hyena_ready")
        x1_ready = sem("x_mixed")
        lg_max, lg_exp, aff_ready = sem("logit_max"), sem("logit_exp"), sem("affinity_ready")
        ht_ready, sel_ready = sem("h_by_token"), sem("selection_ready")
        xs_ready, ct_ready = sem("chosen_ready"), sem("combine_ready")
        xcur_ready = sem("group_chosen_ready")
        gate_done, up_done, down_done = sem("gate_done"), sem("up_done"), sem("down_done")
        sg_ready, hid_done = sem("gate_silu_ready"), sem("hidden_done")
        tr_done, hdt_ready = sem("hidden_turned"), sem("hidden_by_feature")
        y_evac, comb_done, comb_free = sem("y_evacuated"), sem("combined"), sem("combine_added")
        names = ("tab2_loaded bias_loaded c_ready c2_ready u_ready projections_ready gate_logits_ready gqa_squares gqa_roots gqa_normed "
                 "gqa_rotated gate_abs gate_log state_arguments state_exp keys_decayed queries_decayed keys_by_token "
                 "level_arguments level_exp level_ready level_used weights_copied gla_weights_ready gla_output "
                 "gla_squares gla_roots max_ready_2 softmax_exp softmax_normed softmax_turned mixed_ready residual_ready "
                 "mean_ready centred centred_squares ln_roots ffn_gate_ready ffn_hidden_ready ffn_all_hidden output_ready stored")
        (s_tab2, s_ww, c_ready, c2_ready, u_ready, proj_ready, zb_ready, gsq_ready, groot_ready, gnorm_ready,
         rope_ready, abs_ready, log_ready, sarg_ready, sexp_ready, khat_ready, qe_ready, ktok_ready,
         lev_arg, lev_exp, lev_ready, lev_used, atc_ready, at_ready, og_ready,
         osq_ready, oroot_ready, nm_ready, pe_ready, pn_ready, pt_ready, o_ready, res_ready,
         mu_ready, cen_ready, csq_ready, lroot_ready, sga_ready, hj_ready, hid2_done, out_ready, s_out) = map(sem, names.split())
        x3_ready, row_ready = sem("x_first_block"), sem("modulation_row_ready")
        xhat_ready = sem("normed_by_tile")

        def cols(w, a, n):
            return w.rearrange("(k p) n -> p k n", p=P)[:, :, a:a + n]

        def rows(w, a, n):
            return w.rearrange("(k p) n -> p k n", p=P)[:, a:a + n, :]

        w_ada, w_in, w_out = I["w_ada"][0], I["w_in"][0], I["w_out"][0]
        stream = [(f"ada{j}", cols(w_ada, 512 * j, 512)) for j in range(12)]
        stream += [(n, cols(w_in, a, 512)) for n, a in (("q", 0), ("k", 512), ("v", 1024), ("o", 1536),
                                                        ("x1", 2064), ("x2", 2576), ("z", 3088))]
        stream += [(f"ada{l}_{j}", cols(I["w_ada_2"][l], 512 * j, 512)) for l in range(2) for j in range(12)]
        stream += [(f"out{j}", cols(w_out, 512 * j, 512)) for j in range(2)]
        n_before = len(stream)
        UNITS = 16
        GROUPS = NE // 4
        moe = []
        for u in range(UNITS):
            moe += [("gate", u), ("up", u)] + ([("down", u - 1)] if u else [])
        moe.append(("down", UNITS - 1))
        moe_done = {"gate": gate_done, "up": up_done, "down": down_done}

        def moe_source(kind, u, i):
            e, f = 4 * i + u // 4, 512 * (u % 4)
            if kind == "down":
                return I["w_down"][0, e, f:f + 512, :].rearrange("(k p) n -> p k n", p=P)
            return I["w_" + kind][0, e].rearrange("(k p) n -> p k n", p=P)[:, :, f:f + 512]

        def moe_slot(m):
            n = n_before + m
            v = ring[:, n % RING, :]
            return (v.rearrange("p (a b) -> p a b", b=D if moe[m][0] == "down" else 512), landed[n % RING], n // RING + 1)


        stream += [("expert", None)] * (GROUPS * len(moe))
        for l in range(2):
            wi, wo = I["w_in_2"][l], I["w_out_2"][l]
            stream += [(n + str(l), cols(wi, a, w)) for n, a, w in
                       (("gl_qkv", 1152, 512), ("gl_g", 1664, 288), ("ga_q", 1952, 384), ("ga_kv", 2336, 256),
                        ("na_q", 0, 384), ("na_k", 384, 384), ("na_v", 768, 384))]
            stream += [(f"wo{j}{l}", cols(wo, 512 * j, 512)) for j in range(2)]
            stream += [(f"fi{j}{l}", I["w_ffn_in_2"][l].rearrange("(k p) (h n) -> p k h n", p=P, h=2)[:, :, :, 256 * j:256 * j + 256])
                       for j in range(11)]
            stream += [(f"fo{m}{l}", I["w_ffn_out_2"][l].rearrange("(k p) n -> p k n", p=P)[:, :, P * m:P * m + P]) for m in range(KD)]

        STREAMS = [[0, 1], [0]]
        RUNS = [[0, 1], [2]]
        LEVELS = [256, 128, 64, 32, 16, 8, 4, 2, 1]
        UNITS2 = [[(kind, h, qt) for kind in ("na", "ga") for h in range(6) for qt in range(4 - 2 * l)] for l in range(2)]
        NU0 = len(UNITS2[0])

        landing, count = [], [0] * RING
        for n, (name, src) in enumerate(stream):
            count[n % RING] += 32 if name[:2] == "fi" else 16
            landing.append(count[n % RING])

        def slot(n, src):
            a = src.shape[1]
            b = int(np.prod(src.shape[2:]))
            return ring[:, n % RING, 0:a * b].rearrange("p (a b) -> p a b", b=b)

        freed = []

        ADA1 = [("ada", j) for j in range(12)]
        ADA2 = [(f"ada{l}_", j) for l in range(2) for j in range(12)]

        def ada_steps(tiles, rows, turn):
            at_step = [0]

            def take_steps(count=1):
                for _ in range(count):
                    i = at_step[0]
                    at_step[0] += 1
                    assert i <= len(tiles)
                    if i < len(tiles):
                        rows(*tiles[i])
                    if i:
                        turn(*tiles[i - 1])
            return take_steps

        def pe_second(pe, take, release, release_with):
            mm, tr = nc.tensor.matmul, nc.tensor.transpose
            for l in range(2):
                L = str(l)
                nq = (2 - l) * T
                def fm(name, w, c, n, width=P, src=U, kt=KD, modulated=None):
                    b = open_bank(pe, name + L)
                    for k in range(kt):
                        if modulated is not None:
                            pe.wait_ge(u_ready, KD * modulated + k + 1)
                        m = mm(b[0:width, 0:n], w[:, k, c:c + width], src[:, k, 0:n], start=(k == 0), stop=(k == kt - 1))
                    close_bank(m, name + L)

                def tm(name, w, c, width, t, b, o):
                    for k in range(KD):
                        m = mm(b[:, o:o + width], U[:, k, P * t:P * t + P], w[:, k, c:c + width], start=(k == 0), stop=(k == KD - 1))
                    return m

                w = take("gl_qkv" + L)
                fm("gl_q", w, 0, nq, modulated=2 * l)
                fm("gl_k", w, P, 2 * T)
                for t in range(0, 4, 2):
                    b = open_bank(pe, f"gl_v{t}{L}")
                    for i in range(2):
                        m = tm("gl_v", w, 2 * P, T, t + i, b, T * i)
                    close_bank(m, f"gl_v{t}{L}")
                release_with(f"gl_v2{L}")
                w = take("gl_g" + L)
                fm("gl_g0", w, 0, nq)
                fm("gl_g1", w, P, nq)
                fm("gl_lr", w, 2 * P, 2 * T, 32)
                release_with("gl_lr" + L)
                w = take("ga_q" + L)
                for c in range(3):
                    fm(f"ga_q{c}", w, P * c, nq)
                release_with("ga_q2" + L)
                w = take("ga_kv" + L)
                fm("ga_k0", w, 0, 2 * T)
                b = open_bank(pe, "ga_k1" + L)
                for i in range(2):
                    for k in range(KD):
                        m = mm(b[64 * i:64 * i + 64, :], w[:, k, 64 * (1 - i):64 * (1 - i) + 64], U[:, k, :], start=(k == 0), stop=(k == 7))
                close_bank(m, "ga_k1" + L)
                b = open_bank(pe, "ga_v" + L)
                for t in range(4):
                    m = tm("ga_v", w, P, P, t, b, P * t)
                close_bank(m, "ga_v" + L)
                release_with("ga_v" + L)
                for n, width in (("na_q", nq), ("na_k", 2 * T)):
                    w = take(n + L)
                    for c in range(3):
                        fm(f"{n}{c}", w, P * c, width)
                    release_with(f"{n}2{L}")
                w = take("na_v" + L)
                for t in range(4):
                    b = open_bank(pe, f"na_v{t}{L}")
                    close_bank(tm("na_v", w, 0, 384, t, b, 0), f"na_v{t}{L}")
                release_with(f"na_v3{L}")

                pe.wait_ge(proj_ready, l + 1)
                pe.wait_ge(s_tab2, 32)
                for d in range(2):
                    b = open_bank(pe, f"z{d}{L}")
                    close_bank(mm(b[:], wa2[0:32, l, d, :], gllr[0:32, :], start=True, stop=True), f"z{d}{L}")
                for c in range(5):
                    n = nq if c < 3 else 2 * T
                    pe.wait_ge(gsq_ready, 5 * l + c + 1)
                    b = open_bank(pe, f"gn{c}{L}")
                    close_bank(mm(b[:, 0:n], tb2("half64"), gsq[:, c % 2, 0:n], start=True, stop=True), f"gn{c}{L}")
                for c in range(5):
                    pe.wait_ge(gnorm_ready, 5 * l + c + 1)
                    b = open_bank(pe, f"rot{c}{L}")
                    close_bank(mm(b[:, 0:T], tb2("rope_r"), gaq[:, c, 0:T], start=True, stop=True), f"rot{c}{L}")

                pe.wait_ge(khat_ready, l + 1)
                b = open_bank(pe, "kt" + L)
                for d in range(2):
                    for t in range(2):
                        m = tr(b[:, P * (2 * d + t):P * (2 * d + t) + P], khat[:, d, P * t:P * t + P], ident)
                close_bank(m, "kt" + L)
                pe.wait_ge(ktok_ready, l + 1)
                b = open_bank(pe, "S" + L)
                for d in range(2):
                    for t in range(2):
                        m = mm(b[:, T * d:T * d + T], ktok[:, 2 * d + t, :], glv[:, 2 + t, :], start=(t == 0), stop=(t == 1))
                close_bank(m, "S" + L)
                for si, st in enumerate(STREAMS[l]):
                    run = RUNS[l][si]
                    A, Dg = [], []
                    for h in range(4):
                        A.append(open_bank(pe, f"ga{h}{st}{L}"))
                        Dg.append(open_bank(pe, f"gd{h}{st}{L}"))
                    for n, m_ in enumerate(LEVELS):
                        if m_ > 1:
                            pe.wait_ge(lev_ready, 8 * run + n + 1)
                        pairs = []
                        if m_ == 256:
                            pairs = [(P * s, P * (1 - s), P, 0, T * s + P * (1 - s)) for s in range(2)]
                        elif m_ >= 64:
                            q = m_ // 2
                            for blk in range(T // m_):
                                for a in range(2):
                                    s0, t0 = m_ * blk + q * a, m_ * blk + q * (1 - a)
                                    pairs.append((s0, t0, q, s0 % P, T * (s0 // P) + t0))
                        else:
                            for blk in range(8):
                                pairs.append((32 * blk, 32 * blk, 32, 32 * (blk % 4), 192 * (blk // 4) + 32 * (n - 3)))
                        for i, (s0, t0, q, p0, c0) in enumerate(pairs):
                            for h in range(4):
                                hp = slice(32 * h, 32 * h + 32)
                                if m_ > 1:
                                    kh, qh = hat[hp, n % 2, 0, s0:s0 + q], hat[hp, n % 2, 1, t0:t0 + q]
                                else:
                                    kh, qh = glk[hp, T * st + s0:T * st + s0 + q], glq[hp, T * st + t0:T * st + t0 + q]
                                m = mm((A if m_ >= 64 else Dg)[h][p0:p0 + q, c0:c0 + q], kh, qh, start=True, stop=True)
                                if i == len(pairs) - 1 and m_ == 64:
                                    close_bank(m, f"ga{h}{st}{L}")
                                if i == len(pairs) - 1 and m_ == 1:
                                    close_bank(m, f"gd{h}{st}{L}")
                        if m_ not in (64, 1):
                            m.then_inc(lev_used, 1)
                    if st == 0:
                        pe.wait_ge(qe_ready, l + 1)
                    for c in range(2):
                        b = open_bank(pe, f"go{c}{st}{L}")
                        if c == 0:
                            pe.wait_ge(at_ready, run + 1)
                        for i in range(2):
                            for s in range(2):
                                m = mm(b[64 * i:64 * i + 64, 0:T], glv[:, 2 * st + s, 64 * (2 * c + i):64 * (2 * c + i) + 64],
                                       AT[:, 2 * (2 * c + i) + s, :], start=(s == 0), stop=(s == 1))
                        close_bank(m, f"go{c}{st}{L}")
                        if st == 0:
                            b = open_bank(pe, f"gi{c}{L}")
                            for d in range(2):
                                m = mm(b[:, 0:T], S0[:, d, P * c:P * c + P], qe[:, d, :], start=(d == 0), stop=(d == 1))
                            close_bank(m, f"gi{c}{L}")
                pe.wait_ge(osq_ready, l + 1)
                for c in range(2):
                    b = open_bank(pe, f"gls{c}{L}")
                    close_bank(mm(b[:, 0:nq], tb2("half64"), gsq[:, c, 0:nq], start=True, stop=True), f"gls{c}{L}")

                units = UNITS2[l]
                pe.wait_ge(s_ww, 32 * (l + 1))
                pe.wait_ge(rope_ready, l + 1)

                def scores(n):
                    kind, h, qt = units[n]
                    b = open_bank(pe, f"sc{n}{L}")
                    hp = slice(64 * (h % 2), 64 * (h % 2) + 64)
                    keys = slice(0, 2 * T) if qt < 2 else slice(T, 2 * T)
                    q, k = (naq[hp, h // 2], nak[hp, h // 2]) if kind == "na" else \
                           (gaq[hp, h // 2], gaq[hp, 3 + (h // 3 != h % 2)])
                    biased = kind == "na" and qt < 2
                    m = mm(b[:, 0:keys.stop - keys.start], q[:, P * qt:P * qt + P], k[:, keys], start=True, stop=not biased)
                    if biased:
                        at_ = 7 * h + 3 - 2 * qt
                        mm(b[:, 0:T], tb2("flip64"), WW[:, at_:at_ + 4, :], start=False, stop=False)
                        m = mm(b[:, 0:T], ident, bc(tb2("neg_col"), 1, 4, 64), start=False, stop=True)
                    close_bank(m, f"sc{n}{L}")

                def turn(n):
                    kind, h, qt = units[n]
                    pe.wait_ge(pn_ready, NU0 * l + n + 1)
                    b = open_bank(pe, f"pt{n}{L}")
                    for k in range(4 if qt < 2 else 2):
                        m = tr(b[:, P * k:P * k + P], Pr[:, n % 3, P * k:P * k + P], ident)
                    close_bank(m, f"pt{n}{L}")

                def values(n):
                    kind, h, qt = units[n]
                    kts = range(4) if qt < 2 else range(2, 4)
                    pe.wait_ge(pt_ready, NU0 * l + n + 1)
                    b = open_bank(pe, f"ov{n}{L}")
                    hp = slice(64 * (h % 2), 64 * (h % 2) + 64)
                    for i, k in enumerate(kts):
                        v = nav[:, k, 64 * h:64 * h + 64] if kind == "na" else gav[:, k, 64 * (h // 3):64 * (h // 3) + 64]
                        m = mm(b[hp, 0:P], v, PT[:, n % 2, i, :], start=(i == 0), stop=(i == len(kts) - 1))
                    close_bank(m, f"ov{n}{L}")

                nu = len(units)
                for n in range(3):
                    scores(n)
                for n in range(nu):
                    if n + 3 < nu:
                        scores(n + 3)
                    turn(n)
                    if n:
                        values(n - 1)
                values(nu - 1)

                pe.wait_ge(o_ready, l + 1)

                def mean(r, k):
                    pe.wait_ge(res_ready, KD * (2 * l + r) + k + 1)
                    name = f"lm{r}{L}"
                    b = ps[place[name][0]] if k else open_bank(pe, name)
                    m = mm(b[:, 0:nq], ones, XC[:, k, 0:nq], start=(k == 0), stop=(k == KD - 1))
                    if k == KD - 1:
                        close_bank(m, name)

                def variance(r):
                    b = open_bank(pe, f"lv{r}{L}")
                    for k in range(KD):
                        pe.wait_ge(csq_ready, KD * (2 * l + r) + k + 1)
                        m = mm(b[:, 0:nq], ones, U[:, k, 0:nq], start=(k == 0), stop=(k == KD - 1))
                    close_bank(m, f"lv{r}{L}")

                for m_ in range(KD):
                    if m_ % 4 == 0:
                        w = take(f"wo{m_ // 4}{L}")
                    fm(f"wo{m_}_", w, P * (m_ % 4), nq, src=oT)
                    if m_ % 4 == 3:
                        release_with(f"wo{m_}_{L}")
                    if m_:
                        mean(0, m_ - 1)
                mean(0, KD - 1)
                variance(0)
                for j in range(11):
                    w = take(f"fi{j}{L}")
                    for i in range(2):
                        fm(f"fa{2 * j + i}_", w, P * i, nq, modulated=None if j or i else 2 * l + 1)
                        fm(f"fb{2 * j + i}_", w, 2 * P + P * i, nq)
                    release_with(f"fb{2 * j + 1}_{L}")
                pe.wait_ge(hid2_done, l + 1)
                for m_ in range(KD):
                    w = take(f"fo{m_}{L}")
                    fm(f"fo{m_}_", w, 0, nq, src=HID, kt=22)
                    release_with(f"fo{m_}_{L}")
                    if m_:
                        mean(1, m_ - 1)
                mean(1, KD - 1)
                variance(1)

        block = ctx.enter_context(nc.Block())

        @block.tensor
        def _(pe):
            mm = nc.tensor.matmul
            taken = [0]

            def take(name):
                n = taken[0]
                assert stream[n][0] == name, (stream[n][0], name)
                taken[0] += 1
                pe.wait_ge(landed[n % RING], landing[n])
                return slot(n, stream[n][1])

            def release(ins):
                ins.then_inc(drained, 1)
                freed.append((drained, 1 + sum(s is drained for s, _ in freed)))

            def release_with(name):
                b, use = place[name]
                freed.append((full[b], use + 1))

            def fmajor(name, w, j, src, n=256, ktiles=KD):
                b = open_bank(pe, name)
                for i in range(2):
                    for k in range(ktiles):
                        m = mm(b[:, T * i:T * i + T], w[:, k, P * (j + i):P * (j + i) + P], src[:, k, :],
                               start=(k == 0), stop=(k == ktiles - 1))
                close_bank(m, name)
                return m

            def ada_rows(name, j):
                if j == 0 and name == "ada":
                    pe.wait_ge(c_ready, 1)
                if j == 0 and name == "ada0_":
                    pe.wait_ge(c2_ready, 1)
                w = take(f"{name}{j}")
                b = open_bank(pe, f"row_{name}{j}")
                for k in range(KD):
                    g = k % 4
                    m = mm(b[32 * g:32 * g + 32, :], cpad[:, k, :], w[:, k, :], start=(k < 4), stop=(k >= 4))
                close_bank(m, f"row_{name}{j}")
                release_with(f"row_{name}{j}")

            turned = [0]

            def ada_turn(name, j):
                n = 1 if name == "ada" else 2
                turned[0] += 1
                pe.wait_ge(row_ready, turned[0])
                b = open_bank(pe, f"col_{name}{j}")
                for i in range(4):
                    m = mm(b[:, n * i:n * i + n], stages[name][:, j % 2, P * i:P * i + P], tb("pick")[:, 0:n], start=True, stop=True)
                close_bank(m, f"col_{name}{j}")

            ada1, ada2 = ada_steps(ADA1, ada_rows, ada_turn), ada_steps(ADA2, ada_rows, ada_turn)

            pe.wait_ge(s_load, 32)
            pe.wait_ge(s_fil, 96)
            b = open_bank(pe, "hid1")
            close_bank(mm(b[0:64, 0:T], hw1[0:33, :], hfe[0:33, :], start=True, stop=True), "hid1")
            ada1()
            pe.wait_ge(hid_ready, 1)
            b = open_bank(pe, "hid2")
            close_bank(mm(b[0:64, 0:T], hw2[0:64, :], hid[0:64, :], start=True, stop=True), "hid2")
            ada1()
            pe.wait_ge(hid_ready, 2)
            for o in range(2):
                for n in range(TT):
                    for d in range(2):
                        j = 2 * o + d
                        b = open_bank(pe, f"filt{o}{n}{d}")
                        close_bank(mm(b[:], hid2[0:64, P * n:P * n + P], w3[0:64, W * j:W * j + W],
                                       start=True, stop=True), f"filt{o}{n}{d}")
                    ada1()
            for o in range(2):
                pe.wait_ge(ks_ready, 2 * (o + 1))
                for f in range(TT):
                    b = open_bank(pe, f"kre{o}{f}")
                    for n in range(TT):
                        m = mm(b[:], dft["c"][:, n, P * f:P * f + P], KS(o, 0, n),
                               start=(n == 0), stop=(n == 1))
                    close_bank(m, f"kre{o}{f}")
                    b = open_bank(pe, f"kim{o}{f}")
                    for n in range(TT):
                        m = mm(b[:], dft["s"][:, n, P * f:P * f + P], KS(o, 1, n), start=(n == 0), stop=(n == 1 and f == 1))
                    if f == 0:
                        for n in range(TT):
                            m = mm(b[:], dft["n"][:, n, :], KS(o, 0, n), start=False, stop=(n == 1))
                    close_bank(m, f"kim{o}{f}")
                    ada1()
            ada1(3)

            def sums(name, src, count):
                pe.wait_ge(sq_ready, count)
                b = open_bank(pe, name)
                for k in range(KD):
                    m = mm(b[:, 0:T], ones, src[:, k, :], start=(k == 0), stop=(k == KD - 1))
                close_bank(m, name)

            T1v = T1.rearrange("p (a b) -> p a b", b=T)
            sums("ss0", T1v, 1)
            pe.wait_ge(h_ready, 1)
            for n in "qk":
                w = take(n)
                for i in range(2):
                    fmajor(f"{n}{i}", w, 2 * i, hT)
                release_with(f"{n}1")
            w = take("v")
            for t in range(TT):
                b = open_bank(pe, f"v{t}")
                for k in range(KD):
                    m = mm(b[:], hT[:, k, P * t:P * t + P], w[:, k, :], start=(k == 0), stop=(k == 7))
                close_bank(m, f"v{t}")
            release_with("v1")
            w = take("o")
            for i in range(2):
                fmajor(f"o{i}", w, 2 * i, hT)
            release_with("o1")
            pe.wait_ge(s_row, 64)
            b = open_bank(pe, "gates")
            for t in range(TT):
                for k in range(KD):
                    m = mm(b[:, NG * t:NG * t + NG], hT[:, k, P * t:P * t + P], wg[:, k, :], start=(k == 0), stop=(k == 7))
            close_bank(m, "gates")
            for n in ("x1", "x2", "z"):
                w = take(n)
                for i in range(2):
                    fmajor(f"{n}{i}", w, 2 * i, hT)
                release_with(f"{n}1")

            pe.wait_ge(lf_ready, 1)
            b = open_bank(pe, "F")
            for t in range(TT):
                for d in range(2):
                    o = b[:, 8 * t + 4 * d:8 * t + 4 * d + 4]
                    whole = (t == 1) == (d == 0)
                    if whole:
                        mm(o, ones, LF[:, 1 - t, d, :], start=True, stop=False)
                    m = mm(o, tri[d], LF[:, t, d, :], start=not whole, stop=True)
            close_bank(m, "F")
            ada2()
            dg = T1.rearrange("p (t d x) -> p t d x", t=TT, d=2)
            for r, name in ((1, "arow"), (2, "mrow")):
                pe.wait_ge(diag_ready, r)
                for t in range(TT):
                    for d in range(2):
                        b = open_bank(pe, f"{name}{d}{t}")
                        close_bank(mm(b[:], ones, dg[:, t, d, :], start=True, stop=True), f"{name}{d}{t}")
                ada2(2)
            pe.wait_ge(qk_ready, 1)
            for h in range(H):
                b = open_bank(pe, f"s{h}")
                for s in range(TT):
                    m = mm(b[:, T * s:T * s + T], qkT[:, H + h, P * s:P * s + P], qkT[:, h, :], start=True, stop=True)
                close_bank(m, f"s{h}")
            ada2()
            pe.wait_ge(v_ready, 1)
            pe.wait_ge(p_ready, 1)
            for d in range(2):
                for t in range(TT):
                    for hp in range(2):
                        b = open_bank(pe, f"num{d}{t}{hp}")
                        ss = [s for s in range(TT) if (s <= t if d == 0 else s >= t)]
                        for i in range(2):
                            for s in ss:
                                m = mm(b[:, 129 * i:129 * i + 129], E[:, H * (2 * d + s) + 2 * hp + i, P * t:P * t + P],
                                       vtok[:, s, 2 * hp + i, :], start=(s == ss[0]), stop=(s == ss[-1]))
                        close_bank(m, f"num{d}{t}{hp}")
                        ada2()
            pe.wait_ge(hn_ready, 1)
            for t in range(TT):
                b = open_bank(pe, f"ym{t}")
                for h in range(H):
                    m = nc.tensor.transpose(b[:, P * h:P * h + P], hs[:, H * t + h, :], ident)
                close_bank(m, f"ym{t}")
            ada2()

            for o in range(2):
                pe.wait_ge(z_ready, o + 1)
                for t in range(TT):
                    b = open_bank(pe, f"zt{o}{t}")
                    for g in range(4):
                        m = nc.tensor.transpose(b[:, P * g:P * g + P], hxc[:, 8 + g, P * t:P * t + P], ident)
                    close_bank(m, f"zt{o}{t}")
                ada2(2)
                pe.wait_ge(zt_ready, 2 * (o + 1))
                for f in range(TT):
                    b = open_bank(pe, f"ure{o}{f}")
                    for s in range(TT):
                        m = mm(b[:], dft["c"][:, s, P * f:P * f + P], ztok[:, s, :], start=(s == 0), stop=(s == 1))
                    close_bank(m, f"ure{o}{f}")
                    b = open_bank(pe, f"uim{o}{f}")
                    for s in range(TT):
                        m = mm(b[:], dft["s"][:, s, P * f:P * f + P], ztok[:, s, :], start=(s == 0), stop=(s == 1 and f == 1))
                    if f == 0:
                        for s in range(TT):
                            m = mm(b[:], dft["n"][:, s, :], ztok[:, s, :], start=False, stop=(s == 1))
                    close_bank(m, f"uim{o}{f}")
                    ada2()
                pe.wait_ge(y_ready, o + 1)
                for c in range(2):
                    b = open_bank(pe, f"y{o}{c}")
                    for i in range(2):
                        for f in range(TT):
                            for r in range(2):
                                ch = P * (2 * c + i)
                                m = mm(b[:, T * i:T * i + T], Y[:, 2 * r + f, ch:ch + P], idft["cs"[r]][:, f, :],
                                       start=(f == 0 and r == 0), stop=(f == 1 and r == 1))
                    close_bank(m, f"y{o}{c}")
                ada2()
            pe.wait_ge(z_ready, 4)
            for c in range(2):
                b = open_bank(pe, f"hss{c}")
                close_bank(mm(b[:], ones, T1[:, 512 * c:512 * c + 512], start=True, stop=True), f"hss{c}")
            pe.wait_ge(ym_ready, 1)
            pe.wait_ge(yh_ready, 1)
            for j in range(2):
                w = take(f"out{j}")
                for i in range(2):
                    fmajor(f"mix{2 * j + i}", w, 2 * i, yT)
                release_with(f"mix{2 * j + 1}")

            sums("ss1", T1v, 2)
            pe.wait_ge(h_ready, 2)
            b = open_bank(pe, "logit")
            for t in range(TT):
                for k in range(KD):
                    m = mm(b[:, NE * t:NE * t + NE], hT[:, k, P * t:P * t + P], wr[:, k, :], start=(k == 0), stop=(k == 7))
            close_bank(m, "logit")
            for t in range(TT):
                for half in range(2):
                    b = open_bank(pe, f"ht{t}{half}")
                    for k in range(4):
                        m = nc.tensor.transpose(b[:, P * k:P * k + P], hT[:, 4 * half + k, P * t:P * t + P], ident)
                    close_bank(m, f"ht{t}{half}")
            for t in range(TT):
                pe.wait_ge(aff_ready, t + 1)
                for g in range(4):
                    b = open_bank(pe, f"aff{t}{g}")
                    close_bank(mm(b[:], ones, diags[t][:, 4 * g:4 * g + 4, :], start=True, stop=True), f"aff{t}{g}")
            pe.wait_ge(ht_ready, 4)
            pe.wait_ge(sel_ready, 1)
            for k in range(KD):
                b = open_bank(pe, f"xs{k}")
                for t in range(TT):
                    m = mm(b[:], htok[:, t, P * k:P * k + P], sel[:, t].rearrange("p e s -> p (e s)"), start=(t == 0), stop=(t == 1))
                close_bank(m, f"xs{k}")
            for g2 in range(2):
                b = open_bank(pe, f"ct{g2}")
                for i in range(2):
                    for t in range(TT):
                        m = nc.tensor.transpose(b[:, T * i + P * t:T * i + P * t + P],
                                                selg[:, t].rearrange("p e s -> p (e s)")[:, P * (2 * g2 + i):P * (2 * g2 + i) + P], ident)
                close_bank(m, f"ct{g2}")
            pe.wait_ge(xs_ready, 8)
            pe.wait_ge(ct_ready, 2)

            with pe.Fori(0, GROUPS) as i:
                pe.wait_ge(xcur_ready, i + 1)

                def arrive(kind, u):
                    v, s, uses = moe_slot(moe.index((kind, u)))
                    pe.wait_ge(s, i * (16 * len(moe) // RING) + 16 * uses)
                    return v

                def gate_up(u):
                    j = u // 4
                    pe.wait_ge(hid_done, i * UNITS + (u + 1))
                    for kind, bank, done in (("gate", 0, gate_done), ("up", 2, up_done)):
                        w = arrive(kind, u)
                        for k in range(KD):
                            for c in range(4):
                                m = mm(ps[bank + u % 2][32 * c:32 * c + 32, 0:P], xcur[:, k, CAP * j:CAP * j + CAP],
                                       w[:, k, P * c:P * c + P], start=(k == 0), stop=(k == KD - 1))
                        m.then_inc(done, 1)

                def down(u):
                    j, f = u // 4, u % 4
                    pe.wait_ge(hid_done, i * UNITS + (u + 3))
                    nc.tensor.transpose(ps[4][:, 0:P], hidm[:, u % 2, :], ident).then_inc(tr_done, 1)
                    w = arrive("down", u)
                    if u == 0:
                        pe.wait_ge(y_evac, i * 2 + 2)
                    pe.wait_ge(hdt_ready, i * UNITS + (u + 1))
                    for c in range(4):
                        for n in range(2):
                            m = mm(ps[5 + n][CAP * j:CAP * j + CAP, :], hdT[:, u % 2, 32 * c:32 * c + 32], w[:, c, W * n:W * n + W],
                                   start=(f == 0 and c == 0), stop=(f == 3 and c == 3))
                    m.then_inc(down_done, 1)

                gate_up(0)
                for u in range(UNITS):
                    if u + 1 < UNITS:
                        gate_up(u + 1)
                    down(u)
                pe.wait_ge(y_evac, i * 2 + 4)
                for r in range(4):
                    pe.wait_ge(comb_free, i * 4 + (r + 1))
                    for x in range(2):
                        m = mm(ps[7][:, T * x:T * x + T], ysb[:, P * (2 * r + x):P * (2 * r + x) + P], CT[:, i, :], start=True, stop=True)
                    m.then_inc(comb_done, 1)
            pe.wait_ge(comb_free, 4 * GROUPS + 1)
            sums("ssf", T1v, 3)
            for g in range(GROUPS):
                freed.extend((moe_done[kind], UNITS * g + u + 1) for kind, u in moe)
            taken[0] += GROUPS * len(moe)
            pe_second(pe, take, release, release_with)

        def act_mixers(act, step, tell):
            def a(out_, in_, f, **kw):
                return nc.scalar.activation(out_, in_, f, **kw)

            def a_rows(name, j):
                b = read_bank(act, f"row_{name}{j}")
                if j >= 2 or name == "ada1_":
                    read_bank(act, f"col_{name}{j - 2}" if j >= 2 else f"col_ada0_{j + 10}")
                step(a(stages[name][:, j % 2, :], b[:], ACT.Copy), frees=f"row_{name}{j}")
                tell(row_ready)

            ada1, ada2 = (ada_steps(tiles, a_rows, lambda name, j: None) for tiles in (ADA1, ADA2))

            act.wait_ge(s_load, 32)
            for i in range(2):
                if i:
                    ada1()
                act.wait_ge(arg_ready, i + 1)
                step(a((hid, hid2)[i][0:64, :], hid2[0:64, :], ACT.Sin), hid_ready)
            ada1()
            for o in range(2):
                for n in range(TT):
                    for d in range(2):
                        j = 2 * o + d
                        k = (o * TT + n) * 2 + d
                        if k:
                            act.wait_ge(win_used, k)
                        step(a(win, dlt[:, W * j:W * j + W], ACT.Exp, scale=tb("minus_t")[:, n:n + 1]), win_ready)
                    ada1()
            ada1(7)
            act.wait_ge(c_ready, 1)
            step(a(cpad[:, :, 0:2], pc("c2", 0, 16).rearrange("p (k s) -> p k s", s=2), ACT.Silu), c2_ready)

            def root(name, out_, n, k):
                read_bank(act, name)
                step(a(out_, ps[place[name][0]][:, 0:n], ACT.Sqrt, scale=1.0 / D, bias=tb("eps")), frees=name)
                tell(root_ready)

            root("ss0", rs, T, 0)
            for m in range(8):
                name = f"{'qk'[m // 4]}{m // 2 % 2}"
                b = read_bank(act, name)
                i = m % 2
                step(a(qkp[:, m, 1:T + 1], b[:, T * i:T * i + T], ACT.Identity, bias=pc("b_qk", m)),
                     frees=name if i else None)
                if i:
                    tell(qk_evac)
            for m in range(4):
                name = f"o{m // 2}"
                b = read_bank(act, name)
                i = m % 2
                step(a(sgo[:, m, :], b[:, T * i:T * i + T], ACT.Sigmoid, bias=pc("b_o", m)), frees=name if i else None)
            tell(o_evac)
            for m in range(12):
                name = f"{('x1', 'x2', 'z')[m // 4]}{m // 2 % 2}"
                b = read_bank(act, name)
                i = m % 2
                step(a(hxp[:, m, 1:T + 1], b[:, T * i:T * i + T], ACT.Identity, bias=pc("b_hx", m)),
                     frees=name if i else None)
            tell(hx_evac)
            act.wait_ge(g_ready, 1)
            step(a(LG, AB, ACT.Exp, scale=-1.0))
            step(a(LG, LG, ACT.Ln, bias=1.0), g_ln)
            ada2()
            act.wait_ge(conv_ready, 1)
            step(a(qkT, qkT, ACT.Silu), qk_ready)
            ada2(2)
            act.wait_ge(mx_ready, 1)
            step(a(EM, EM, ACT.Exp, scale=-1.0), em_ready)
            ada2(2)
            act.wait_ge(e_arg, 1)
            for g in range(4):
                lo, hi = ((0, T), (P, T), (0, P), (0, T))[g]
                step(a(E[:, H * g:H * g + H, lo:hi], E[:, H * g:H * g + H, lo:hi], ACT.Exp, scale=-1.0), e_ready)
            ada2(9)
            act.wait_ge(hs_ready, 1)
            for j in range(8):
                step(a(T1[:, P * j:P * j + P], hs[:, j, :], ACT.Square, accum_out=sst[:, j:j + 1]))
            step(a(rst, sst, ACT.Sqrt, scale=1.0 / P, bias=tb("eps")), ss_ready)
            ada2()
            for o in range(2):
                for t in range(TT):
                    name = f"zt{o}{t}"
                    b = read_bank(act, name)
                    step(a(ztok[:, t, :], b[:], ACT.Copy), frees=name)
                    tell(zt_ready)
                ada2(5)
            for c in range(2):
                name = f"hss{c}"
                b = read_bank(act, name)
                step(a(T1[:, 1024 + 512 * c:1536 + 512 * c], b[:], ACT.Sqrt, scale=1.0 / P, bias=tb("eps")), frees=name)
            tell(root_ready)


        def act_moe(act, step, tell):
            a = nc.scalar.activation

            def root(name):
                b = read_bank(act, name)
                step(a(rs, b[:, 0:T], ACT.Sqrt, scale=1.0 / D, bias=tb("eps")), frees=name)
                tell(root_ready)

            root("ss1")
            for t in range(TT):
                for half in range(2):
                    b = read_bank(act, f"ht{t}{half}")
                    step(a(htok[:, t, 512 * half:512 * half + 512], b[:], ACT.Copy), frees=f"ht{t}{half}")
                    tell(ht_ready)
            act.wait_ge(lg_max, 1)
            step(a(logit, logit, ACT.Exp), lg_exp)
            for k in range(KD):
                b = read_bank(act, f"xs{k}")
                step(a(xs[:, k, :], b[:], ACT.Copy), frees=f"xs{k}")
                tell(xs_ready)
            for g2 in range(2):
                b = read_bank(act, f"ct{g2}")
                step(a(CT[:, 2 * g2:2 * g2 + 2, :], b[:].rearrange("p (a b) -> p a b", a=2), ACT.Copy), frees=f"ct{g2}")
                tell(ct_ready)
            with act.Fori(0, GROUPS) as i:
                def silu(u):
                    act.wait_ge(gate_done, i * UNITS + (u + 1))
                    a(sg[:, u % 2, :], ps[u % 2][:, 0:P], ACT.Silu).then_inc(sg_ready, 1)

                silu(0)
                for u in range(UNITS):
                    if u + 1 < UNITS:
                        silu(u + 1)
                    act.wait_ge(tr_done, i * UNITS + (u + 1))
                    a(hdT[:, u % 2, :], ps[4][:, 0:P], ACT.Copy).then_inc(hdt_ready, 1)
            root("ssf")

        def modulated(dve, step, tell, gain, scale, shift, k, src):
            v = nc.vector
            tt, ts, stt = v.tensor_tensor, v.tensor_scalar, v.scalar_tensor_tensor
            T1v = T1.rearrange("p (a b) -> p a b", b=T)
            step(tt(T1v, src, src, ALU.mult), sq_ready)
            step(stt(out=A1, in0=scale, scalar=1.0, in1=gain, op0=ALU.add, op1=ALU.mult))
            dve.wait_ge(root_ready, k)
            step(v.reciprocal(rs, rs))
            for j in range(KD):
                step(stt(out=hT[:, j, :], in0=src[:, j, :], scalar=A1[:, j:j + 1], in1=rs, op0=ALU.mult, op1=ALU.mult))
                step(ts(hT[:, j, :], hT[:, j, :], shift[:, j:j + 1], None, ALU.add))
            tell(h_ready)

        def dve_mixers(dve, step, tell):
            v = nc.vector
            tt, ts, stt = v.tensor_tensor, v.tensor_scalar, v.scalar_tensor_tensor

            def turned(name, j):
                b = read_bank(dve, f"col_{name}{j}")
                if name == "ada":
                    step(tt(mod[:, 4 * j:4 * j + 4], b[:, 0:4], pc("b_ada", 4 * j, 4), ALU.add), frees=f"col_{name}{j}")
                else:
                    l = int(name[3])
                    step(tt(mod2early[:, l, 4 * j:4 * j + 4, :], b[:, 0:8].rearrange("p (j s) -> p j s", s=2),
                            bc(pc(f"b_ada_{l}", 4 * j, 4), 2, 4, 2), ALU.add), frees=f"col_{name}{j}")

            ada1, ada2 = (ada_steps(tiles, lambda name, j: None, turned) for tiles in (ADA1, ADA2))
            dve.wait_ge(s_load, 32)
            step(v.memset(cpad, 0.0))
            step(v.tensor_copy(cpad[:, :, 0], pc("c", 0, 8)), c_ready)

            dve.wait_ge(s_fil, 96)
            for i in range(2):
                b = read_bank(dve, f"hid{i + 1}")
                if i:
                    ada1()
                    dve.wait_ge(hid_ready, 1)
                bb, fr = hhp[0:64, 1 + i:2 + i], hhp[0:64, 0:1]
                x, y = hid2[0:64, :], T1[0:64, 0:T]
                step(ts(x, b[0:64, 0:T], bb, fr, ALU.add, ALU.mult), frees=f"hid{i + 1}")
                step(ts(y, x, 1 / (2 * np.pi), None, ALU.mult))
                step(ts(y, y, 1.5 * 2 ** 23, None, ALU.add))
                step(ts(y, y, -1.5 * 2 ** 23, None, ALU.add))
                for part in TWO_PI:
                    step(stt(out=x, in0=y, scalar=-part, in1=x, op0=ALU.mult, op1=ALU.add))
                step(ts(x, x, 3.1415925, -3.1415925, ALU.min, ALU.max), arg_ready)
            ada1()
            for o in range(2):
                for n in range(TT):
                    for d in range(2):
                        name = f"filt{o}{n}{d}"
                        b = read_bank(dve, name)
                        k = (o * TT + n) * 2 + d
                        dve.wait_ge(win_ready, k + 1)
                        step(stt(out=hwt[:, d, :], in0=win, scalar=0.05, in1=b[:], op0=ALU.add, op1=ALU.mult), frees=name)
                        tell(win_used)
                    step(tt(KS(o, 0, n), hwt[:, 0, :], hwt[:, 1, :], ALU.add))
                    step(tt(KS(o, 1, n), hwt[:, 0, :], hwt[:, 1, :], ALU.subtract), ks_ready)
                    ada1()
            for o in range(2):
                for f in range(TT):
                    r, m = KR[:, 2 * o + f, :], KI[:, 2 * o + f, :]
                    b = read_bank(dve, f"kre{o}{f}")
                    step(v.tensor_copy(r, b[:]), frees=f"kre{o}{f}")
                    b = read_bank(dve, f"kim{o}{f}")
                    step(v.tensor_copy(m, b[:]), frees=f"kim{o}{f}")
                    if f == 0:
                        step(ts(KB[:, o, :], r, tb("keep_im"), None, ALU.mult))
                        step(stt(out=KB[:, o, :], in0=m, scalar=tb("swap_im"), in1=KB[:, o, :], op0=ALU.mult, op1=ALU.add))
                        step(ts(m, m, tb("keep_im"), None, ALU.mult))
                    ada1()
            T1v = T1.rearrange("p (a b) -> p a b", b=T)
            ada1(3)
            dve.wait_ge(s_x, 16)
            modulated(dve, step, tell, pc("g_mix", 0, 8), mod[:, 8:16], mod[:, 0:8], 1, xT)
            dve.wait_ge(s_row, 64)
            step(v.memset(vtok, 1.0))
            for pad in (qkp, hxp):
                for e in (0, T + 1):
                    step(v.memset(pad[:, :, e:e + 1], 0.0))

            def conv(dst, src, wname, bname, m, n):
                step(ts(dst, src[:, 0:T], pc(wname, m), pc(bname, m), ALU.mult, ALU.add))
                for j in (1, 2):
                    step(stt(out=dst, in0=src[:, j:j + T], scalar=pc(wname, n * j + m), in1=dst, op0=ALU.mult, op1=ALU.add))

            for m in range(8):
                dve.wait_ge(qk_evac, m // 2 + 1)
                conv(qkT[:, m, :], qkp[:, m, :], "conv_qk_w", "conv_qk_b", m, 8)
            tell(conv_ready)
            for t in range(TT):
                b = read_bank(dve, f"v{t}")
                step(tt(vtok[:, t, :, 0:P], b[:].rearrange("p (h d) -> p h d", h=H), bv.rearrange("p (h d) -> p h d", h=H), ALU.add),
                     frees=f"v{t}")
            tell(v_ready)
            b = read_bank(dve, "gates")
            step(tt(G, b[:, 0:32].rearrange("p (t g) -> p t g", t=TT), bc(bg, 1, TT, NG), ALU.add), frees="gates")
            Gv = G.rearrange("p t (d k h) -> p t d k h", d=2, k=2)
            for t in range(TT):
                step(v.tensor_copy(FI[:, t], Gv[:, t, :, 1, :]))
            fi, ab = (x.rearrange("p t d h -> p (t d h)") for x in (FI, AB))
            step(stt(out=ab, in0=fi, scalar=-1.0, in1=fi, op0=ALU.mult, op1=ALU.max))
            tell(g_ready)
            dve.wait_ge(g_ln, 1)
            step(stt(out=LF, in0=FI, scalar=0.0, in1=LG, op0=ALU.min, op1=ALU.subtract), lf_ready)
            dve.wait_ge(hx_evac, 1)
            for m in range(12):
                conv(hxc[:, m, :], hxp[:, m, :], "conv_hy_w", "conv_hy_b", m, 12)
            tell(z_ready)
            b = read_bank(dve, "F")
            F4 = b[:, 0:16].rearrange("p (t d h) -> p t d h", t=TT, d=2)
            for t in range(TT):
                step(tt(AC[:, t], Gv[:, t, :, 0, :], F4[:, t], ALU.subtract))
            step(v.tensor_copy(FI, F4), frees="F")
            ada2()

            def diagonals(src):
                for t in range(TT):
                    d8 = T1[:, 1024 * t:1024 * t + 1024].rearrange("p (j x) -> p j x", j=8)
                    s8 = src[:, t].rearrange("p d h -> p (d h)")
                    step(tt(d8, bc(ident, 1, 8, P), bc(s8, 2, 8, P), ALU.mult))
                tell(diag_ready)

            diagonals(AC)
            for t in range(TT):
                for d in range(2):
                    name = f"arow{d}{t}"
                    b3 = read_bank(dve, name)[:].rearrange("p (h s) -> p h s", h=H)
                    if (t == 0) == (d == 0):
                        step(v.tensor_reduce(MF[:, 1 - t, d, :], b3, AX.X, ALU.max))
                    e3 = E[:, 0:H, 0:P]
                    step(tt(e3, b3, bc(neg[d], 1, H, P), ALU.add), frees=name)
                    step(v.tensor_reduce(MD[:, t, d, :], e3, AX.X, ALU.max))
            ada2(2)
            step(v.tensor_copy(MX, MD))
            step(tt(MX[:, 1, 0, :], MX[:, 1, 0, :], MF[:, 1, 0, :], ALU.max))
            step(tt(MX[:, 0, 1, :], MX[:, 0, 1, :], MF[:, 0, 1, :], ALU.max))
            step(tt(EM, FI, MX, ALU.add), mx_ready)
            diagonals(MX)
            for t in range(TT):
                for d in range(2):
                    name = f"mrow{d}{t}"
                    b3 = read_bank(dve, name)[:].rearrange("p (h s) -> p h s", h=H)
                    for s in range(TT):
                        if (s > t) if d == 0 else (s < t):
                            continue
                        g = 2 * d + s
                        e3 = E[:, H * g:H * g + H, P * t:P * t + P]
                        last = s == (1 if (d == 1 or t == 1) else 0)
                        step(tt(e3, b3, bc(AC[:, s, d, :], 2, H, P), ALU.subtract), frees=name if last else None)
                        if s == t:
                            step(ts(e3, e3, 0.0, None, ALU.max))
            ada2(2)
            tell(e_arg)
            dve.wait_ge(e_ready, 4)
            for t in range(TT):
                for d in range(2):
                    g = 2 * d + t
                    e3 = E[:, H * g:H * g + H, P * t:P * t + P]
                    step(tt(e3, e3, bc(tri[d], 1, H, P), ALU.mult))
            for h in range(H):
                b = read_bank(dve, f"s{h}")
                for g in range(4):
                    lo, hi = ((0, T), (P, T), (0, P), (0, T))[g]
                    s = g % 2
                    e = E[:, H * g + h, lo:hi]
                    step(stt(out=e, in0=b[:, T * s + lo:T * s + hi], scalar=P ** -0.5, in1=e, op0=ALU.mult, op1=ALU.mult),
                         frees=f"s{h}" if g == 3 else None)
            tell(p_ready)
            ada2()
            dve.wait_ge(em_ready, 1)
            for d in range(2):
                for t in range(TT):
                    for hp in range(2):
                        name = f"num{d}{t}{hp}"
                        b3 = read_bank(dve, name)[:, 0:258].rearrange("p (i x) -> p i x", i=2)
                        den = b3[:, :, P]
                        step(v.tensor_copy(dn[:, 2:4], den))
                        step(stt(out=dn[:, 0:2], in0=dn[:, 2:4], scalar=-1.0, in1=dn[:, 2:4], op0=ALU.mult, op1=ALU.max))
                        step(tt(dn[:, 0:2], dn[:, 0:2], EM[:, t, d, 2 * hp:2 * hp + 2], ALU.max))
                        step(v.reciprocal(dn[:, 0:2], dn[:, 0:2]))
                        for i in range(2):
                            o = hs[:, H * t + 2 * hp + i, :]
                            fr = name if i else None
                            if d == 0:
                                step(ts(o, b3[:, i, 0:P], dn[:, i:i + 1], None, ALU.mult), frees=fr)
                            else:
                                step(stt(out=o, in0=b3[:, i, 0:P], scalar=dn[:, i:i + 1], in1=o, op0=ALU.mult, op1=ALU.add), frees=fr)
                        ada2()
            tell(hs_ready)
            dve.wait_ge(ss_ready, 1)
            step(v.reciprocal(rst, rst))
            step(tt(hs, hs, bc(rst, 2, 8, P), ALU.mult), hn_ready)
            dve.wait_ge(o_evac, 1)
            for t in range(TT):
                b = read_bank(dve, f"ym{t}")
                for h in range(H):
                    step(stt(out=yT[:, h, P * t:P * t + P], in0=b[:, P * h:P * h + P], scalar=pc("mlstm_norm_g", h),
                             in1=sgo[:, h, P * t:P * t + P], op0=ALU.mult, op1=ALU.mult), frees=f"ym{t}" if h == 3 else None)
            tell(ym_ready)
            ada2()
            ta, tc = T1[:, 0:W], T1[:, W:2 * W]
            for o in range(2):
                ada2(2)
                for f in range(TT):
                    re, im = read_bank(dve, f"ure{o}{f}"), read_bank(dve, f"uim{o}{f}")
                    kr, ki = KR[:, 2 * o + f, :], KI[:, 2 * o + f, :]
                    kb = KB[:, o, :] if f == 0 else kr
                    step(tt(ta, kr, re[:], ALU.mult))
                    step(tt(tc, ki, im[:], ALU.mult))
                    step(tt(Y[:, f, :], ta, tc, ALU.subtract))
                    step(tt(ta, kb, im[:], ALU.mult), frees=f"uim{o}{f}")
                    step(tt(tc, ki, re[:], ALU.mult), frees=f"ure{o}{f}")
                    step(tt(Y[:, 2 + f, :], ta, tc, ALU.add))
                    ada2()
                tell(y_ready)
                for c in range(2):
                    b = read_bank(dve, f"y{o}{c}")
                    for i in range(2):
                        g = 2 * c + i
                        z = hxc[:, 8 + g, :]
                        step(stt(out=z, in0=z, scalar=pc("hy_bias", 4 * o + g), in1=b[:, T * i:T * i + T], op0=ALU.mult, op1=ALU.add),
                             frees=f"y{o}{c}" if i else None)
                        step(tt(z, z, hxc[:, 4 * o + g, :], ALU.mult))
                tell(z_ready)
                ada2()
            z4 = hxc[:, 8:12, :]
            t4 = T1[:, 0:1024].rearrange("p (g t) -> p g t", g=4)
            step(tt(t4, z4, z4, ALU.mult), z_ready)
            dve.wait_ge(root_ready, 2)
            r4 = T1[:, 1024:2048].rearrange("p (g t) -> p g t", g=4)
            step(v.reciprocal(r4, r4))
            for g in range(4):
                step(stt(out=yT[:, 4 + g, :], in0=z4[:, g, :], scalar=pc("hyena_norm_g", g), in1=r4[:, g, :], op0=ALU.mult, op1=ALU.mult))
            tell(yh_ready)
            for j in range(4):
                b = read_bank(dve, f"mix{j}")
                for i in range(2):
                    m = 2 * j + i
                    step(stt(out=xT[:, m, :], in0=b[:, T * i:T * i + T], scalar=mod[:, 16 + m:17 + m], in1=xT[:, m, :],
                             op0=ALU.mult, op1=ALU.add), frees=f"mix{j}" if i else None)

        def dve_moe(dve, step, tell):
            v = nc.vector
            tt, ts, stt = v.tensor_tensor, v.tensor_scalar, v.scalar_tensor_tensor
            modulated(dve, step, tell, pc("g_ffn", 0, 8), mod[:, 32:40], mod[:, 24:32], 3, xT)
            b = read_bank(dve, "logit")
            step(v.tensor_copy(logit, b[:, 0:2 * NE].rearrange("p (t e) -> p t e", t=TT)), frees="logit")
            step(v.tensor_reduce(rmx, logit, AX.X, ALU.max))
            step(tt(logit, logit, bc(rmx, 2, TT, NE), ALU.subtract), lg_max)
            dve.wait_ge(lg_exp, 1)
            step(v.tensor_reduce(rsm, logit, AX.X, ALU.add))
            step(v.reciprocal(rsm, rsm))
            step(tt(aff, logit, bc(rsm, 2, TT, NE), ALU.mult))
            for t in range(TT):
                step(tt(diags[t], bc(ident, 1, NE, P), bc(aff[:, t, :], 2, NE, P), ALU.mult), aff_ready)
            for j in range(TT):
                for g in range(4):
                    name = f"aff{j}{g}"
                    R = read_bank(dve, name)[:].rearrange("p (e t) -> p e t", e=4)
                    for i in range(TT):
                        mine = bc(aff[:, i, 4 * g:4 * g + 4], 2, 4, P)
                        fr = name if i else None
                        if i == j:
                            step(tt(cmp2, R, mine, ALU.is_equal))
                            step(tt(cmp2, cmp2, bc(tb("before"), 1, 4, P), ALU.mult))
                        step(tt(cmp_, R, mine, ALU.is_ge if j < i else ALU.is_gt), frees=fr)
                        if i == j:
                            step(tt(cmp_, cmp_, cmp2, ALU.add))
                        step(v.tensor_reduce(rpart[:, j, i, 4 * g:4 * g + 4], cmp_, AX.X, ALU.add))
            step(tt(rank, rpart[:, 0], rpart[:, 1], ALU.add))
            for t in range(TT):
                step(tt(sel[:, t], bc(rank[:, t, :], 2, NE, CAP), bc(tb("slots"), 1, NE, CAP), ALU.is_equal))
                step(tt(selg[:, t], sel[:, t], bc(aff[:, t, :], 2, NE, CAP), ALU.mult))
            tell(sel_ready)
            for s, k in ((hid_done, 2), (y_evac, 2), (comb_free, 1)):
                for _ in range(k):
                    dve.sem_inc(s, 1)
            dve.wait_ge(xs_ready, 8)
            with dve.Fori(0, GROUPS) as i:
                v.tensor_copy(xcur, xs[:, :, bass.ts(i, P)]).then_inc(xcur_ready, 1)
                for u in range(UNITS):
                    dve.wait_ge(sg_ready, i * UNITS + (u + 1))
                    dve.wait_ge(up_done, i * UNITS + (u + 1))
                    tt(hidm[:, u % 2, :], sg[:, u % 2, :], ps[2 + u % 2][:, 0:P], ALU.mult).then_inc(hid_done, 1)
                dve.wait_ge(down_done, i * UNITS + UNITS)
                for n in range(2):
                    v.tensor_copy(ysb[:, W * n:W * n + W], ps[5 + n][:]).then_inc(y_evac, 1)
                for r in range(4):
                    dve.wait_ge(comb_done, i * 4 + (r + 1))
                    for x in range(2):
                        m = 2 * r + x
                        ins = stt(out=xT[:, m, :], in0=ps[7][:, T * x:T * x + T], scalar=mod[:, 40 + m:41 + m], in1=xT[:, m, :],
                                  op0=ALU.mult, op1=ALU.add)
                    ins.then_inc(comb_free, 1)
            dve.wait_ge(comb_free, 4 * GROUPS + 1)
            step(tt(T1.rearrange("p (a b) -> p a b", b=T), xT, xT, ALU.mult), sq_ready)
            dve.wait_ge(root_ready, 4)
            step(v.reciprocal(rs, rs))
            step(v.tensor_copy(mod2s, mod2early))
            step(ts(A2, mod2s[:, 0, 8:16, :], 1.0, None, ALU.add))
            step(v.tensor_copy(B2, mod2s[:, 0, 0:8, :]))
            for j in range(KD):
                step(stt(out=xT[:, j, :], in0=xT[:, j, :], scalar=pc("g_final", j), in1=rs, op0=ALU.mult, op1=ALU.mult), x3_ready)

        def act_second(act, step, tell):
            a = nc.scalar.activation

            def evac(name, dst, f=ACT.Copy, n=None, width=P, **kw):
                b = read_bank(act, name)
                src = b[0:width, 0:n] if n else b[:]
                if len(dst.shape) == 3:
                    src = src.rearrange("p (a b) -> p a b", a=dst.shape[1])
                step(a(dst, src, f, **kw), frees=name)

            def modulate(k, streams):
                for s in range(streams):
                    r = slice(T * s, T * s + T)
                    step(a(U[:, k, r], XC[:, k, r], ACT.Identity, scale=A2[:, k, s:s + 1], bias=B2[:, k, s:s + 1]))
                tell(u_ready)

            act.wait_ge(s_x, 32)
            for k in range(KD):
                act.wait_ge(x3_ready, k + 1)
                modulate(k, 2)
            for l in range(2):
                L = str(l)
                nq = (2 - l) * T
                evac("gl_q" + L, glq[:, 0:nq], n=nq, scale=32 ** -0.5)
                evac("gl_k" + L, glk)
                for t in range(0, 4, 2):
                    evac(f"gl_v{t}{L}", glv[:, t:t + 2, :])
                for c in range(2):
                    evac(f"gl_g{c}{L}", glg[:, c, 0:nq], ACT.Silu, n=nq)
                evac("gl_lr" + L, gllr[0:32, :], n=2 * T, width=32)
                for c in range(3):
                    evac(f"ga_q{c}{L}", gaq[:, c, 0:nq], n=nq)
                for c in range(2):
                    evac(f"ga_k{c}{L}", gaq[:, 3 + c, :])
                evac("ga_v" + L, gav)
                for c in range(3):
                    evac(f"na_q{c}{L}", naq[:, c, 0:nq], n=nq, scale=0.125)
                for c in range(3):
                    evac(f"na_k{c}{L}", nak[:, c, :])
                for t in range(4):
                    evac(f"na_v{t}{L}", nav[:, t, :], n=384)
                tell(proj_ready)
                for d in range(2):
                    evac(f"z{d}{L}", la[:, d, :], ACT.Identity, bias=pc("gla_ba_" + L, d))
                tell(zb_ready)
                def square(c):
                    n = nq if c < 3 else 2 * T
                    step(a(gsq[:, c % 2, 0:n], gaq[:, c, 0:n], ACT.Square), gsq_ready)

                square(0)
                square(1)
                for c in range(5):
                    n = nq if c < 3 else 2 * T
                    if c >= 2:
                        act.wait_ge(gnorm_ready, 5 * l + c - 1)
                    evac(f"gn{c}{L}", grt[:, c % 2, 0:n], ACT.Sqrt, n=n, scale=1 / 64, bias=tb("eps"))
                    tell(groot_ready)
                    if c + 2 < 5:
                        square(c + 2)
                act.wait_ge(abs_ready, l + 1)
                step(a(AB2, AB2, ACT.Exp, scale=-1.0))
                step(a(AB2, AB2, ACT.Ln, bias=1.0), log_ready)
                act.wait_ge(sarg_ready, l + 1)
                step(a(sarg, sarg, ACT.Exp), sexp_ready)
                evac("kt" + L, ktok)
                tell(ktok_ready)
                for si, st in enumerate(STREAMS[l]):
                    run = RUNS[l][si]
                    for n in range(8):
                        act.wait_ge(lev_arg, 8 * run + n + 1)
                        step(a(ex[:, n % 2, :], ex[:, n % 2, :], ACT.Exp), lev_exp)
                    if run:
                        act.wait_ge(og_ready, run)
                    for h in range(4):
                        evac(f"ga{h}{st}{L}", AT[:, 2 * h:2 * h + 2, :])
                        tell(atc_ready)
                act.wait_ge(og_ready, RUNS[l][-1] + 1)
                for c in range(2):
                    step(a(gsq[:, c, 0:nq], og[:, c, 0:nq], ACT.Square))
                tell(osq_ready)
                for c in range(2):
                    evac(f"gls{c}{L}", grt[:, c, 0:nq], ACT.Sqrt, n=nq, scale=1 / 64, bias=tb("eps"))
                tell(oroot_ready)

                units = UNITS2[l]
                nu = len(units)

                def soft(n):
                    kind, h, qt = units[n]
                    nk = 2 * T if qt < 2 else T
                    act.wait_ge(nm_ready, NU0 * l + n + 1)
                    b = read_bank(act, f"sc{n}{L}")
                    step(a(Pr[:, n % 3, 0:nk], b[:, 0:nk], ACT.Exp, scale=1.0 if kind == "na" else 0.125,
                           bias=nm[:, n % 4:n % 4 + 1], accum_out=sm[:, n % 4:n % 4 + 1]), frees=f"sc{n}{L}")
                    tell(pe_ready)

                for n in range(2):
                    soft(n)
                for n in range(nu):
                    nk = 4 if units[n][2] < 2 else 2
                    b = read_bank(act, f"pt{n}{L}")
                    step(a(PT[:, n % 2, 0:nk, :], b[:, 0:P * nk].rearrange("p (a b) -> p a b", a=nk), ACT.Copy), frees=f"pt{n}{L}")
                    tell(pt_ready)
                    if n + 2 < nu:
                        soft(n + 2)

                def norm_roots(r):
                    evac(f"lm{r}{L}", mu[:, 0:nq], n=nq, scale=1.0 / D)
                    tell(mu_ready)
                    n = 2 * l + r
                    for k in range(KD):
                        act.wait_ge(cen_ready, KD * n + k + 1)
                        step(a(U[:, k, 0:nq], XC[:, k, 0:nq], ACT.Square), csq_ready)
                    evac(f"lv{r}{L}", rs2[:, 0:nq], ACT.Sqrt, n=nq, scale=1.0 / D, bias=tb("ln_eps"))
                    tell(lroot_ready)
                    if n < 3:
                        for k in range(KD):
                            act.wait_ge(xhat_ready, KD * n + k + 1)
                            modulate(k, nq // T)

                norm_roots(0)
                for j in range(22):
                    if j >= 2:
                        act.wait_ge(hj_ready, 22 * l + j - 1)
                    evac(f"fa{j}_{L}", sga[:, j % 2, 0:nq], ACT.Silu, n=nq)
                    tell(sga_ready)
                norm_roots(1)

        def dve_second(dve, step, tell):
            v = nc.vector
            tt, ts, stt = v.tensor_tensor, v.tensor_scalar, v.scalar_tensor_tensor
            dve.wait_ge(s_x, 32)
            for l in range(2):
                L = str(l)
                nq = (2 - l) * T
                mod2 = mod2s[:, l]

                if l == 0:
                    for k in range(KD):
                        dve.wait_ge(u_ready, k + 1)
                        step(ts(XC[:, k, :], XC[:, k, :], ALPHA, None, ALU.mult))
                dve.wait_ge(zb_ready, l + 1)
                dve.wait_ge(s_tab2, 32)
                step(stt(out=AB2, in0=la, scalar=-1.0, in1=la, op0=ALU.mult, op1=ALU.max), abs_ready)
                for c in range(5):
                    n = nq if c < 3 else 2 * T
                    dve.wait_ge(groot_ready, 5 * l + c + 1)
                    step(v.reciprocal(grt[:, c % 2, 0:n], grt[:, c % 2, 0:n]))
                    w = pc(("qnorm_" if c < 3 else "knorm_") + L)
                    step(stt(out=gaq[:, c, 0:n], in0=gaq[:, c, 0:n], scalar=w, in1=grt[:, c % 2, 0:n], op0=ALU.mult, op1=ALU.mult), gnorm_ready)
                for c in range(5):
                    b = read_bank(dve, f"rot{c}{L}")
                    step(tt(rtmp, b[:, 0:T], tb2("rope_s"), ALU.mult), frees=f"rot{c}{L}")
                    x = gaq[:, c, 0:T]
                    step(tt(x, x, tb2("rope_c"), ALU.mult))
                    step(tt(x, x, rtmp, ALU.add))
                tell(rope_ready)
                dve.wait_ge(log_ready, l + 1)
                step(stt(out=la, in0=la, scalar=0.0, in1=AB2, op0=ALU.min, op1=ALU.subtract))
                step(ts(la, la, 1 / 16, None, ALU.mult))
                for d in range(2):
                    for s in range(2):
                        r = slice(T * s, T * s + T)
                        o, i = B[:, d, r], la[:, d, r]
                        if d:
                            o, i = o[:, ::-1], i[:, ::-1]
                        step(v.tensor_tensor_scan(o, ones[:, 0:1].to_broadcast([P, T]), i, 0.0, ALU.mult, ALU.add))
                for d in range(2):
                    last = B[:, d, 2 * T - 1:2 * T] if d == 0 else B[:, d, T:T + 1]
                    step(tt(sarg[:, d, :], last.to_broadcast([P, T]), B[:, d, T:2 * T], ALU.subtract))
                    step(v.tensor_copy(sarg[:, 2 + d, :], B[:, d, 0:T]))
                tell(sarg_ready)
                dve.wait_ge(sexp_ready, l + 1)
                step(tt(khat, khat, bc(glk[:, T:2 * T], 1, 2, T), ALU.mult), khat_ready)
                step(tt(qe, qe, bc(glq[:, 0:T], 1, 2, T), ALU.mult), qe_ready)
                b = read_bank(dve, "S" + L)
                step(tt(S0, b[:].rearrange("p (d x) -> p d x", d=2), bc(tb2("gla_bd"), 1, 2, T), ALU.mult), frees="S" + L)
                for si, st in enumerate(STREAMS[l]):
                    run = RUNS[l][si]
                    b0, b1 = B[:, 0, T * st:T * st + T], B[:, 1, T * st:T * st + T]

                    def args(n):
                        m = LEVELS[n]
                        h = m // 2
                        c, d, ek, eq = (x.rearrange("p (n m) -> p n m", m=m) for x in (b0, b1, ex[:, n % 2, 0:T], ex[:, n % 2, T:2 * T]))
                        mid0, mid1 = (bc(x, 2, T // m, h) for x in (c[:, :, h - 1], d[:, :, h]))
                        step(tt(ek[:, :, 0:h], mid0, c[:, :, 0:h], ALU.subtract))
                        step(tt(ek[:, :, h:m], mid1, d[:, :, h:m], ALU.subtract))
                        step(tt(eq[:, :, 0:h], d[:, :, 0:h], mid1, ALU.subtract))
                        step(tt(eq[:, :, h:m], c[:, :, h:m], mid0, ALU.subtract), lev_arg)

                    args(0)
                    for n in range(8):
                        if n + 1 < 8:
                            args(n + 1)
                        dve.wait_ge(lev_exp, 8 * run + n + 1)
                        if n >= 2:
                            if LEVELS[n - 2] == 64:
                                read_bank(dve, f"ga3{st}{L}")
                            else:
                                dve.wait_ge(lev_used, 7 * run + n - 1 - (n - 2 > 2))
                        e2 = ex[:, n % 2, :].rearrange("p (a b) -> p a b", a=2)
                        step(tt(hat[:, n % 2, 0, :], e2[:, 0, :], glk[:, T * st:T * st + T], ALU.mult))
                        step(tt(hat[:, n % 2, 1, :], e2[:, 1, :], glq[:, T * st:T * st + T], ALU.mult), lev_ready)
                    for h in range(4):
                        name = f"gd{h}{st}{L}"
                        b = read_bank(dve, name)
                        lv = dgt[:, 0:384].rearrange("p (t x) -> p t x", t=2)
                        step(tt(lv, b[:, 0:384].rearrange("p (t x) -> p t x", t=2), bc(lvmask, 1, 2, 192), ALU.mult), frees=name)
                        lr = dgt[:, 384:448].rearrange("p (t x) -> p t x", t=2)
                        step(v.tensor_reduce(lr, lv.rearrange("p t (v x) -> p t x v", v=6), AX.X, ALU.add))
                        dve.wait_ge(atc_ready, 4 * run + h + 1)
                        for t in range(2):
                            for j in range(4):
                                q = slice(32 * j, 32 * j + 32)
                                c = P * t + 32 * j
                                step(v.tensor_copy(AT[q, 2 * h + t, c:c + 32], lr[q, t, :]))
                    tell(at_ready)
                    for c in range(2):
                        b = read_bank(dve, f"go{c}{st}{L}")
                        o = og[:, c, T * st:T * st + T]
                        step(v.tensor_copy(o, b[:, 0:T]), frees=f"go{c}{st}{L}")
                        if st == 0:
                            b = read_bank(dve, f"gi{c}{L}")
                            step(tt(o, o, b[:, 0:T], ALU.add), frees=f"gi{c}{L}")
                    tell(og_ready)
                dve.wait_ge(oroot_ready, l + 1)
                for c in range(2):
                    r, o = grt[:, c, 0:nq], og[:, c, 0:nq]
                    step(v.reciprocal(r, r))
                    step(stt(out=o, in0=o, scalar=pc("gla_norm_" + L), in1=r, op0=ALU.mult, op1=ALU.mult))
                    step(tt(oT[:, 3 + c, 0:nq], o, glg[:, c, 0:nq], ALU.mult))

                units = UNITS2[l]
                nu = len(units)

                def largest(n):
                    kind, h, qt = units[n]
                    nk = 2 * T if qt < 2 else T
                    b = read_bank(dve, f"sc{n}{L}")
                    m = nm[:, n % 4:n % 4 + 1]
                    step(v.tensor_reduce(m, b[:, 0:nk], AX.X, ALU.max))
                    step(ts(m, m, -1.0 if kind == "na" else -0.125, None, ALU.mult), nm_ready)

                def output(n):
                    kind, h, qt = units[n]
                    b = read_bank(dve, f"ov{n}{L}")
                    hp = slice(64 * (h % 2), 64 * (h % 2) + 64)
                    step(v.tensor_copy(oT[hp, (0 if kind == "na" else 5) + h // 2, P * qt:P * qt + P], b[hp, 0:P]), frees=f"ov{n}{L}")

                def normed(n):
                    nk = 2 * T if units[n][2] < 2 else T
                    dve.wait_ge(pe_ready, NU0 * l + n + 1)
                    s_ = sm[:, n % 4:n % 4 + 1]
                    step(v.reciprocal(s_, s_))
                    step(ts(Pr[:, n % 3, 0:nk], Pr[:, n % 3, 0:nk], s_, None, ALU.mult), pn_ready)

                largest(0)
                largest(1)
                normed(0)
                for n in range(nu):
                    if n + 1 < nu:
                        normed(n + 1)
                    if n + 2 < nu:
                        largest(n + 2)
                    if n > 1:
                        output(n - 2)
                output(nu - 2)
                output(nu - 1)
                tell(o_ready)

                def residual(name, gate):
                    for m in range(KD):
                        b = read_bank(dve, f"{name}{m}_{L}")
                        for s in range(nq // T):
                            r = slice(T * s, T * s + T)
                            step(stt(out=XC[:, m, r], in0=b[:, r], scalar=mod2[:, gate + m, s:s + 1], in1=XC[:, m, r], op0=ALU.mult, op1=ALU.add),
                                 frees=f"{name}{m}_{L}" if s == nq // T - 1 else None)
                        tell(res_ready)

                def layer_norm(r):
                    n = 2 * l + r
                    bias = pc(f"ln{r + 1}_b_{L}", 0, 8)
                    dve.wait_ge(mu_ready, n + 1)
                    for m in range(KD):
                        step(tt(XC[:, m, 0:nq], XC[:, m, 0:nq], mu[:, 0:nq], ALU.subtract), cen_ready)
                    if n < 3:
                        ahead, base = (l, 24) if r == 0 else (l + 1, 0)
                        step(ts(A2, mod2s[:, ahead, base + 8:base + 16, :], 1.0, None, ALU.add))
                        step(tt(B2, A2, bc(bias, 2, KD, 2), ALU.mult))
                        step(tt(B2, B2, mod2s[:, ahead, base:base + 8, :], ALU.add))
                        step(ts(AB_, bias, ALPHA, None, ALU.mult))
                    dve.wait_ge(lroot_ready, n + 1)
                    step(v.reciprocal(rs2[:, 0:nq], rs2[:, 0:nq]))
                    for m in range(KD):
                        x = XC[:, m, 0:nq]
                        step(stt(out=x, in0=x, scalar=pc(f"ln{r + 1}_g_{L}", m), in1=rs2[:, 0:nq], op0=ALU.mult, op1=ALU.mult), xhat_ready)
                    for m in range(KD):
                        x = XC[:, m, 0:nq]
                        if n < 3:
                            dve.wait_ge(u_ready, KD * (n + 1) + m + 1)
                            step(ts(x, x, ALPHA, AB_[:, m:m + 1], ALU.mult, ALU.add))
                        else:
                            step(ts(x, x, pc(f"ln{r + 1}_b_{L}", m), None, ALU.add))

                residual("wo", 16)
                layer_norm(0)
                for j in range(22):
                    dve.wait_ge(sga_ready, 22 * l + j + 1)
                    b = read_bank(dve, f"fb{j}_{L}")
                    step(tt(HID[:, j, 0:nq], sga[:, j % 2, 0:nq], b[:, 0:nq], ALU.mult), frees=f"fb{j}_{L}")
                    tell(hj_ready)
                tell(hid2_done)
                residual("fo", 40)
                layer_norm(1)
            tell(out_ready)

        @block.scalar
        def _(act):
            step, tell = chain(act, act_own)
            act_mixers(act, step, tell)
            act_moe(act, step, tell)
            act_second(act, step, tell)

        @block.vector
        def _(dve):
            step, tell = chain(dve, dve_own)
            dve_mixers(dve, step, tell)
            dve_moe(dve, step, tell)
            dve_second(dve, step, tell)

        @block.gpsimd
        def _(pool):
            pool.wait_ge(out_ready, 1)

        @block.sync
        def _(sp):
            for dst, src in ((hw1[0:33, :], I["hy_w1"][0]), (hw2[0:64, :], I["hy_w2"][0]), (hfe[0:33, :], I["features"]),
                             (w3[0:64, :], I["hy_w3"][0]), (hhp[0:64, 0:3], I["hy_cols"]),
                             (dlt, I["hy_deltas"].to_broadcast([P, 4 * W]))):
                sp.dma_start(dst, src).then_inc(s_fil, 16)
            sp.dma_start(par[:], I["params"]).then_inc(s_load, 16)
            sp.dma_start(tab[:], I["tables1"]).then_inc(s_load, 16)
            sp.dma_start(xT, I["xT"].rearrange("(k p) t -> p k t", p=P)).then_inc(s_x, 16)

            def load(n):
                if n >= RING:
                    sp.wait_ge(*freed[n - RING])
                sp.dma_start(slot(n, stream[n][1]), stream[n][1]).then_inc(landed[n % RING], 16)

            for n in range(RING):
                load(n)
            sp.dma_start(bv, I["b_v"].to_broadcast([P, W])).then_inc(s_row, 16)
            sp.dma_start(bg, I["b_gates"].to_broadcast([P, NG])).then_inc(s_row, 16)
            sp.dma_start(wg, cols(w_in, 4 * W, NG)).then_inc(s_row, 16)
            sp.dma_start(wr, cols(I["w_router"][0], 0, NE)).then_inc(s_row, 16)
            for n in range(RING, n_before):
                load(n)

            def load_moe(m, i, ahead=0):
                v, s, _ = moe_slot(m)
                kind, u = moe[m - RING]
                before = (m < RING)
                if ahead or not before:
                    sp.wait_ge(moe_done[kind], i * UNITS + (u + 1))
                sp.dma_start(v, moe_source(*moe[m], i + ahead)).then_inc(s, 16)

            sp.dma_start(XC[:, :, T:2 * T], I["ctxT"].rearrange("(k p) t -> p k t", p=P)).then_inc(s_x, 16)
            for m in range(RING):
                sp.wait_ge(*freed[n_before - RING + m])
                load_moe(m, 0)
            with sp.Fori(0, GROUPS - 1) as i:
                for m in range(RING, len(moe)):
                    load_moe(m, i)
                for m in range(RING):
                    load_moe(m, i, 1)
            for m in range(RING, len(moe)):
                load_moe(m, GROUPS - 1)

            for n in range(n_before + GROUPS * len(moe), len(stream)):
                name, src = stream[n]
                if name == "na_q0":
                    sp.wait_ge(x3_ready, KD)
                    sp.dma_start(arena[:, 0:n_tab2], I["tables2"]).then_inc(s_tab2, 16)
                    sp.dma_start(wa2[0:32], I["gla_wa2"]).then_inc(s_tab2, 16)
                if name in ("na_q0", "gl_qkv1"):
                    l = int(name[-1])
                    if l:
                        sp.wait_ge(o_ready, 1)
                    for half in range(2):
                        src_ = bass.AP(I["rpb"].tensor, (l * 42) * P, [[1, 64], [P, 42 - half], [1, 64]])
                        sp.dma_start(WW[64 * half:64 * half + 64, half:42, :], src_).then_inc(s_ww, 16)
                sp.wait_ge(*freed[n - RING])
                v = slot(n, src)
                if len(src.shape) == 4:
                    for h in range(2):
                        sp.dma_start(v[:, :, 256 * h:256 * h + 256], src[:, :, h, :]).then_inc(landed[n % RING], 16)
                else:
                    sp.dma_start(v, src).then_inc(landed[n % RING], 16)
            sp.wait_ge(out_ready, 1)
            sp.dma_start(out.rearrange("(k p) t -> p k t", p=P), xT).then_inc(s_out, 16)
            sp.wait_ge(s_out, 16)


_DIRECT = ["w_ada", "w_in", "w_out", "hy_w1", "hy_w2", "hy_w3", "hy_deltas", "w_router", "w_gate", "w_up", "w_down",
           "w_ada_2", "w_in_2", "w_out_2", "w_ffn_in_2", "w_ffn_out_2"]


def kernel_arrays(inputs):
    a = {n: np.ascontiguousarray(inputs[n]) for n in _DIRECT}

    def c(x, reps=1):
        x = np.tile(np.asarray(x).reshape(-1), reps)
        return x.reshape(-1, P).T

    i = inputs
    b_in = np.asarray(i["b_in"])[0]
    one = {"c": i["c"], "b_qk": b_in[0:1024], "b_o": b_in[1536:2048], "b_hx": b_in[2064:3600]}
    parts = [c(one[n] if n in one else i[n]) for n, _ in COLS1]
    c2 = np.stack([c(i["c_2"]), c(i["c_ctx_2"])], -1).reshape(P, 16)
    parts.append(c2)
    two = {"gla_norm": ("gla_norm_w_2", 2), "qnorm": ("gqa_qnorm_w_2", 2), "knorm": ("gqa_knorm_w_2", 2), "gla_ba": ("gla_ba_2", 1)}
    for l in range(2):
        for n, _ in COLS2:
            src, reps = two.get(n, (n + "_2", 1))
            parts.append(c(np.asarray(i[src])[l], reps))
    a["params"] = np.ascontiguousarray(np.concatenate(parts, 1))
    a["tables1"], a["tables2"] = tables()
    a["features"] = features()
    a["hy_cols"] = np.ascontiguousarray(np.stack([np.asarray(i[n])[0] for n in ("hy_freq", "hy_b1", "hy_b2")], 1))
    a["b_v"] = np.ascontiguousarray(b_in[None, 1024:1536])
    a["b_gates"] = np.ascontiguousarray(b_in[None, 2048:2064])
    rpb = np.asarray(i["na_rpb_2"])[:, :, 4:11, :].reshape(2, 42, 31)
    a["rpb"] = np.ascontiguousarray(np.pad(rpb, ((0, 0), (0, 0), (48, P - 79))))
    w = np.asarray(i["gla_wa2_2"])
    wa = np.stack([np.pad(w[:, d], ((0, 0), (16 * d, 16 - 16 * d), (0, 0))) for d in range(2)], 1)
    a["gla_wa2"] = np.ascontiguousarray(wa.transpose(2, 0, 1, 3))
    a["xT"] = np.ascontiguousarray(np.asarray(i["x"])[0].T)
    a["ctxT"] = np.ascontiguousarray(np.asarray(i["ctx_2"])[0].T)
    return a


def kernel(**inputs):
    import concourse.bacc as bacc
    from concourse.bass_utils import run_bass_kernel_spmd

    nc = bacc.Bacc("TRN2", target_bir_lowering=False, num_devices=1)
    arrays = kernel_arrays(inputs)
    aps = {n: nc.dram_tensor(f"in_{n}", a.shape, mybir.dt.from_np(a.dtype), kind="ExternalInput").ap()
           for n, a in arrays.items()}
    out = nc.dram_tensor("out", (D, T), F32, kind="ExternalOutput").ap()
    build(nc, aps, out)
    r = run_bass_kernel_spmd(nc, [{f"in_{n}": a for n, a in arrays.items()}], core_ids=[0])
    return np.ascontiguousarray(r.results[0]["out"].T)[None]
```
